# Optimizing a Trainium2 kernel written in Bass

```python
import jax, jax.numpy as jnp
from jax import lax
import numpy as np

D_MODEL = 1024
BATCH = 1
SEQ = 256
DEPTH = 2

CHUNK = 64
CONV_W = 512
CONV_K = 31
SGU_W = 512
SGU_GROUPS = 4
SGU_CHUNK = 128
ATTN_HEADS = 8
ATTN_HEAD_DIM = 64
ATTN_W = ATTN_HEADS * ATTN_HEAD_DIM
ATTN_LEFT_CHUNKS = 8
ATTN_BAND = (ATTN_LEFT_CHUNKS + 1) * CHUNK
REL_MIN = -(CHUNK - 1)
REL_MAX = 128
N_REL = REL_MAX - REL_MIN + 1
N_BRANCH = 3
N_IN = 2 * CONV_W + 2 * SGU_W + 3 * ATTN_W + N_BRANCH * D_MODEL
D_FF = 2816
N_EXPERTS = 8
TOP_K = 2
D_FF_EXPERT = 3584
N_DENSE = (DEPTH + 1) // 2
N_MOE = DEPTH // 2
EPS = 1e-6
NEG_INF = -1e30

kernel_name = "hybrid_conv_sgu_chunkattn_moe_trunk"

def rms_norm(x, g):
    xf = x.astype(jnp.float32)
    y = xf * lax.rsqrt(jnp.mean(xf * xf, axis=-1, keepdims=True) + EPS)
    return (y * g.astype(jnp.float32)).astype(x.dtype)

def layer_norm(x, g, b):
    xf = x.astype(jnp.float32)
    mu = jnp.mean(xf, axis=-1, keepdims=True)
    var = jnp.mean(jnp.square(xf - mu), axis=-1, keepdims=True)
    y = (xf - mu) * lax.rsqrt(var + EPS) * g.astype(jnp.float32) + b.astype(jnp.float32)
    return y.astype(x.dtype)

def conv_branch(a, dw_w, dw_b, ln_g, ln_b, out_w):
    h = a[..., :CONV_W] * jax.nn.sigmoid(a[..., CONV_W:])
    h = lax.conv_general_dilated(
        h, dw_w[:, None, :], window_strides=(1,), padding=[(CONV_K - 1, 0)],
        dimension_numbers=("NWC", "WIO", "NWC"), feature_group_count=CONV_W) + dw_b
    h = jax.nn.silu(layer_norm(h, ln_g, ln_b))
    return h @ out_w

def sgu_branch(a, ws, bs, ln_g, ln_b, out_w):
    b, s, _ = a.shape
    a = jax.nn.gelu(a, approximate=False)
    u, v = a[..., :SGU_W], a[..., SGU_W:]
    v = layer_norm(v, ln_g, ln_b)
    n = s // SGU_CHUNK
    v = v.reshape(b, n, SGU_CHUNK, SGU_GROUPS, SGU_W // SGU_GROUPS)
    pos = jnp.arange(SGU_CHUNK)
    mask = (pos[None, :] // CHUNK) <= (pos[:, None] // CHUNK)
    w = jnp.where(mask[None], ws, jnp.zeros_like(ws))
    mixed = jnp.einsum("gts,bnsgc->bntgc", w, v) + bs.T[:, :, None]
    return (u * mixed.reshape(b, s, SGU_W)) @ out_w

def attn_branch(a, rel_table, out_w):
    b, s, _ = a.shape
    nc = s // CHUNK
    shp = (b, nc, CHUNK, ATTN_HEADS, ATTN_HEAD_DIM)
    q = a[..., :ATTN_W].reshape(shp)
    k = a[..., ATTN_W:2 * ATTN_W].reshape(shp)
    v = a[..., 2 * ATTN_W:].reshape(shp)
    pad = ((0, 0), (ATTN_LEFT_CHUNKS, 0), (0, 0), (0, 0), (0, 0))
    kp, vp = jnp.pad(k, pad), jnp.pad(v, pad)
    k_band = jnp.concatenate([kp[:, j:j + nc] for j in range(ATTN_LEFT_CHUNKS + 1)], axis=2)
    v_band = jnp.concatenate([vp[:, j:j + nc] for j in range(ATTN_LEFT_CHUNKS + 1)], axis=2)
    scores = jnp.einsum("bnqhd,bnkhd->bnhqk", q, k_band,
                        preferred_element_type=jnp.float32) * (ATTN_HEAD_DIM ** -0.5)
    qi = jnp.arange(CHUNK)
    kj = jnp.arange(ATTN_BAND)
    rel = ATTN_LEFT_CHUNKS * CHUNK + qi[:, None] - kj[None, :]
    idx = jnp.clip(rel, REL_MIN, REL_MAX) - REL_MIN
    bias = rel_table.astype(jnp.float32)[:, idx]
    key_chunk = jnp.arange(nc)[:, None] - ATTN_LEFT_CHUNKS + kj[None, :] // CHUNK
    valid = key_chunk >= 0
    add = jnp.where(valid[:, None, None, :], bias[None], NEG_INF)
    p = jax.nn.softmax(scores + add[None], axis=-1).astype(v.dtype)
    o = jnp.einsum("bnhqk,bnkhd->bnqhd", p, v_band)
    return o.reshape(b, s, ATTN_W) @ out_w

def swiglu(x, wg, wu, wd):
    return (jax.nn.silu(x @ wg) * (x @ wu)) @ wd

def moe_swiglu(x, router, wg, wu, wd):
    b, s, d = x.shape
    t = x.reshape(b * s, d)
    logits = jnp.dot(t, router, preferred_element_type=jnp.float32)
    top_v, top_i = lax.top_k(logits, TOP_K)
    top_w = jax.nn.softmax(top_v, axis=-1)
    combine = jnp.sum(jax.nn.one_hot(top_i, N_EXPERTS, dtype=jnp.float32) * top_w[..., None], axis=1)
    combine = combine.astype(t.dtype)
    out = jnp.zeros_like(t)
    for e in range(N_EXPERTS):
        out = out + combine[:, e:e + 1] * swiglu(t, wg[e], wu[e], wd[e])
    return out.reshape(b, s, d)

def setup_inputs(seed: int = 0) -> dict:
    key = jax.random.key(seed)
    ks = iter(jax.random.split(key, 32))

    def nrm(shape, scale):
        return jax.random.normal(next(ks), shape, jnp.float32) * scale

    L, D = DEPTH, D_MODEL
    return {
        "x": nrm((BATCH, SEQ, D), 1.0),
        "mix_norm_g": 1.0 + nrm((L, D), 0.02),
        "w_in": nrm((L, D, N_IN), D ** -0.5),
        "b_gate": nrm((L, N_BRANCH * D), 0.02),
        "conv_dw_w": nrm((L, CONV_K, CONV_W), CONV_K ** -0.5),
        "conv_dw_b": nrm((L, CONV_W), 0.02),
        "conv_ln_g": 1.0 + nrm((L, CONV_W), 0.02),
        "conv_ln_b": nrm((L, CONV_W), 0.02),
        "conv_out_w": nrm((L, CONV_W, D), CONV_W ** -0.5),
        "sgu_ln_g": 1.0 + nrm((L, SGU_W), 0.02),
        "sgu_ln_b": nrm((L, SGU_W), 0.02),
        "sgu_ws": nrm((L, SGU_GROUPS, SGU_CHUNK, SGU_CHUNK), SGU_CHUNK ** -0.5),
        "sgu_bs": 1.0 + nrm((L, SGU_GROUPS, SGU_CHUNK), 0.02),
        "sgu_out_w": nrm((L, SGU_W, D), SGU_W ** -0.5),
        "attn_rel_bias": nrm((L, ATTN_HEADS, N_REL), 0.1),
        "attn_out_w": nrm((L, ATTN_W, D), ATTN_W ** -0.5),
        "w_out": nrm((L, D, D), D ** -0.5),
        "ffn_norm_g": 1.0 + nrm((L, D), 0.02),
        "ffn_w_gate": nrm((N_DENSE, D, D_FF), D ** -0.5),
        "ffn_w_up": nrm((N_DENSE, D, D_FF), D ** -0.5),
        "ffn_w_down": nrm((N_DENSE, D_FF, D), D_FF ** -0.5),
        "moe_router": nrm((N_MOE, D, N_EXPERTS), D ** -0.5),
        "moe_w_gate": nrm((N_MOE, N_EXPERTS, D, D_FF_EXPERT), D ** -0.5),
        "moe_w_up": nrm((N_MOE, N_EXPERTS, D, D_FF_EXPERT), D ** -0.5),
        "moe_w_down": nrm((N_MOE, N_EXPERTS, D_FF_EXPERT, D), D_FF_EXPERT ** -0.5),
        "final_norm_g": 1.0 + nrm((D,), 0.02),
    }

def reference(x, mix_norm_g, w_in, b_gate, conv_dw_w, conv_dw_b, conv_ln_g, conv_ln_b,
              conv_out_w, sgu_ln_g, sgu_ln_b, sgu_ws, sgu_bs, sgu_out_w, attn_rel_bias,
              attn_out_w, w_out, ffn_norm_g, ffn_w_gate, ffn_w_up, ffn_w_down, moe_router,
              moe_w_gate, moe_w_up, moe_w_down, final_norm_g):
    o1 = 2 * CONV_W
    o2 = o1 + 2 * SGU_W
    o3 = o2 + 3 * ATTN_W
    h = x
    for layer in range(DEPTH):
        xn = rms_norm(h, mix_norm_g[layer])
        a = xn @ w_in[layer]
        y_conv = conv_branch(a[..., :o1], conv_dw_w[layer], conv_dw_b[layer],
                             conv_ln_g[layer], conv_ln_b[layer], conv_out_w[layer])
        y_sgu = sgu_branch(a[..., o1:o2], sgu_ws[layer], sgu_bs[layer],
                           sgu_ln_g[layer], sgu_ln_b[layer], sgu_out_w[layer])
        y_attn = attn_branch(a[..., o2:o3], attn_rel_bias[layer], attn_out_w[layer])
        g = jax.nn.sigmoid(a[..., o3:] + b_gate[layer])
        merged = (g[..., :D_MODEL] * y_conv
                  + g[..., D_MODEL:2 * D_MODEL] * y_sgu
                  + g[..., 2 * D_MODEL:] * y_attn)
        h = h + merged @ w_out[layer]
        xn = rms_norm(h, ffn_norm_g[layer])
        i = layer // 2
        if layer % 2 == 0:
            h = h + swiglu(xn, ffn_w_gate[i], ffn_w_up[i], ffn_w_down[i])
        else:
            h = h + moe_swiglu(xn, moe_router[i], moe_w_gate[i], moe_w_up[i], moe_w_down[i])
    return rms_norm(h, final_norm_g)


_drawn_inputs = setup_inputs


def setup_inputs(seed=0):
    import zlib

    import numpy as np

    out = dict(_drawn_inputs(seed))
    spreads = {}
    factors = {'b_gate': 4.015, 'attn_rel_bias': 3.887, 'final_norm_g': 2.814}
    for name, (base, spread) in spreads.items():
        noise = np.random.default_rng([zlib.crc32(name.encode()), seed]).standard_normal(out[name].shape)
        drawn = base * np.exp(spread * noise) if base else spread * noise
        out[name] = __import__('jax').numpy.asarray(drawn.astype(out[name].dtype))
    for name, factor in factors.items():
        out[name] = (out[name] * factor).astype(out[name].dtype)
    return out
```

```python
from contextlib import ExitStack

import concourse.bass as bass
from concourse import mybir

F32 = mybir.dt.float32
F32R = mybir.dt.float32r
I32 = mybir.dt.int32
U32 = mybir.dt.uint32
ACT = mybir.ActivationFunctionType
ALU = mybir.AluOpType
AX = mybir.AxisListType

P = 128
D, T, L = 1024, 256, 2
KD, NT = D // P, T // P
CW, TAPS, CG = 512, 31, 4
HEADS, HD = 8, 64
CHUNK, N_REL = 64, 192
FT = 2816 // P
NE, FE = 8, 3584
NJ = FE // 512
EPS = 1e-6
NEG = -1e30
RSQRT_SEED = float(0x5F3759DF)

UNIT = 1024
RAW, SPLIT, AHEAD = 12, 6, 5
MIX_UNITS, FFN_UNITS, MOE_UNITS = 72, 3 * FT, 12 * NJ
MIX_A, FFN_A = 44, 2 * FT
MIX_BASE = [0, MIX_UNITS + FFN_UNITS]
FFN_BASE = MIX_UNITS
MOE_BASE = MIX_BASE[1] + MIX_UNITS
A_BASE = [0, MIX_A + FFN_A]
FFN_A_BASE = MIX_A
MOE_A_USES = (A_BASE[1] + MIX_A) // 2
Y_USES = 9
BRANCH_UNIT = [28, 40, 52]
BRANCH_GATE = [8, 0, 16]
SLOT_OF_HEAD = [28 + 2 * h for h in range(HEADS)]

C_MIXG, C_GATEB, C_CONVW, C_CONVB, C_LNG, C_LNB, C_FFNG = 0, 8, 32, 156, 160, 164, 168
C_LAYER = 176


def at(constant, turn, stride):
    return constant if turn is None else turn * stride + constant


class Order:

    def __init__(self, eng, sem):
        self.eng, self.sem, self.n, self.turn, self.stride = eng, sem, 0, None, 0

    def value(self, back=0):
        return at(self.n - back, self.turn, self.stride)

    def mark(self, ins):
        ins.then_inc(self.sem, 1)
        self.n += 1

    def link(self, ins):
        self.mark(ins)
        self.eng.wait_ge(self.sem, self.value())

    def enter(self, turn, stride):
        self.turn, self.stride, self.at_entry = turn, stride, self.n

    def leave(self, turns):
        assert self.n - self.at_entry == self.stride, (self.n - self.at_entry, self.stride)
        self.n = self.at_entry + self.stride * turns
        self.turn, self.stride = None, 0


def trunk(nc, x, w_in, conv_out_w, sgu_out_w, attn_out_w, w_out, ffn_w_gate, ffn_w_up, ffn_w_down,
          moe_router, moe_w_gate, moe_w_up, moe_w_down, params, sgu_ln_g, sgu_ln_b, sgu_wsT, sgu_bs,
          rel_reversed, ffn_norm_g, final_norm_g, out):
    with ExitStack() as ctx:
        def sb(name, shape, dt=F32):
            return ctx.enter_context(nc.sbuf_tensor(name, shape, dt))

        def sem(name):
            return ctx.enter_context(nc.semaphore(name))

        raw = sb("raw", [P, RAW, UNIT])
        whi = sb("whi", [P, SPLIT, UNIT], F32R)
        wlo = sb("wlo", [P, SPLIT, UNIT], F32R)

        x_hi = sb("x_hi", [P, 2048], F32R)
        x_lo = sb("x_lo", [P, 2048], F32R)
        br_ab = sb("br_ab", [P, 4096], F32R)
        br_c = sb("br_c", [P, 2048], F32R)
        xT_hi = x_hi[:, :].rearrange("p (k t) -> p k t", k=KD)
        xT_lo = x_lo[:, :].rearrange("p (k t) -> p k t", k=KD)

        def quarter(a, n, k):
            return a[:, n * 1024:(n + 1) * 1024].rearrange("p (k t) -> p k t", k=k)

        sgu_hi, sgu_lo = quarter(br_ab, 0, 4), quarter(br_ab, 1, 4)
        conv_hi, conv_lo = quarter(br_ab, 2, 4), quarter(br_ab, 3, 4)
        attn_hi, attn_lo = quarter(br_c, 0, 4), quarter(br_c, 1, 4)
        branch_parts = [(sgu_hi, sgu_lo), (conv_hi, conv_lo), (attn_hi, attn_lo)]
        mrg_hi = br_ab[:, 0:2048].rearrange("p (k t) -> p k t", k=KD)
        mrg_lo = br_ab[:, 2048:4096].rearrange("p (k t) -> p k t", k=KD)
        fh_hi = br_c[:, 0:512].rearrange("p (b t) -> p b t", b=2)
        fh_lo = br_c[:, 512:1024].rearrange("p (b t) -> p b t", b=2)
        tok_hi = x_hi[:, :].rearrange("p (i d) -> p i d", i=NT)
        tok_lo = x_lo[:, :].rearrange("p (i d) -> p i d", i=NT)
        slot_parts = [quarter(br_ab, 0, KD), quarter(br_ab, 1, KD)]
        ye_hi, ye_lo = br_ab[:, 2048:3072], br_ab[:, 3072:4096]
        eh_hi = br_c[:, 0:512].rearrange("p (k t) -> p k t", k=4)
        eh_lo = br_c[:, 512:1024].rearrange("p (k t) -> p k t", k=4)
        pick = br_c[:, 1024:1280].rearrange("p (i s) -> p i s", i=NT)
        pickT = br_c[:, 1280:1536]

        h = sb("h", [P, NT, D])
        xn = sb("xn", [P, 2048])
        xn_tok = xn[:, :].rearrange("p (i d) -> p i d", i=NT)
        merged = xn[:, :].rearrange("p (k t) -> p k t", k=KD)
        cin = sb("cin", [P, CG, TAPS - 1 + T])
        cacc = sb("cacc", [P, CG, T])
        uT = sb("uT", [P, 4, T])
        gate_t = uT[:, :, :].rearrange("p (b m) t -> p b m t", b=2)
        v_sgu = sb("v_sgu", [P, 1024])
        v_tok = v_sgu[:, :].rearrange("p (i c) -> p i c", i=NT)
        um = v_sgu[:, :].rearrange("p (g t) -> p g t", g=4)
        csq = um
        qT = sb("qT", [P, 4, T])
        kT = sb("kT", [P, 4, T])
        v_att = sb("v_att", [P, NT, ATTN_W := HEADS * HD])
        bias_t = sb("bias_t", [P, HEADS, 2 * P])
        routeT = bias_t[:, :, :]
        probs = sb("probs", [P, 4 * 384])
        S = probs[:, 0:768].rearrange("p (b n) -> p b n", b=2)
        pT = probs[:, 768:1536].rearrange("p (b n) -> p b n", b=2)
        ln_gb = probs[:, 0:1024].rearrange("p (b n) -> p b n", b=2)
        stat = sb("stat", [P, 3, T])
        sig, mtmp = stat[:, 0:2, :], stat[:, 0:2, :]
        tap_act, tap_pool = stat[:, 0:2, :], stat[:, 2, :]
        bs_b = sb("bs_b", [P, 4, P])
        wsT = sb("wsT", [P, 4, P])
        e_sl, e_h = uT[:, 0:2, :].rearrange("p a t -> p (a t)"), uT[:, 2:4, :].rearrange("p a t -> p (a t)")
        f_sl, f_h = uT[:, 0:2, :], uT[:, 2:4, :]
        g_ffn_b = qT[:, :, :].rearrange("p a t -> p (a t)")
        g_fin_b = kT[:, :, :].rearrange("p a t -> p (a t)")

        ident = sb("ident", [P, P])
        anti = sb("anti", [P, P])
        ones = sb("ones", [P, P])
        par = sb("par", [P, L * C_LAYER])
        par_half = sb("par_half", [P, L * C_LAYER])
        small = sb("small", [P, 64])
        router = v_att[:, 0, 0:64].rearrange("p (k e) -> p k e", k=KD)
        upper = v_att[:, 0, 128:256]
        ones1 = v_att[:, 0, 256:384]
        iota = v_att[:, 1, 0:128]
        top = sb("top", [P, NT, 8])
        topi = sb("topi", [P, NT, 8], U32)
        logit = sb("logit", [P, NT, 8])
        flag = sb("flag", [P, 1], I32)
        extv = wsT[0:HEADS, :, :].rearrange("p a b -> p (a b)")
        iota_i = v_att[:, 1, 128:256].bitcast(I32)
        chosen = sb("chosen", [P, NT, NE + 1])
        rank = sb("rank", [P, NT, NE + 1])
        slot = sb("slot", [P, NT, NE + 1])
        weight = sb("weight", [P, NT, NE + 1])
        sel = sb("sel", [P, 2, NE])
        scratch = nc.dram_tensor("rel_rows", (L, HEADS, 384), F32).ap()

        bank = [ctx.enter_context(nc.psum_tensor(f"bank{n}", [P, 512], F32)) for n in range(8)]

        raw_loaded = [sem(f"raw_loaded{n}") for n in range(RAW)]
        hi_made, lo_made, unit_used = sem("hi_made"), sem("lo_made"), sem("unit_used")
        a_read = [sem("bank0_read"), sem("bank1_read")]
        y_read = [sem("bank2_read"), sem("bank3_read")]
        x_loaded, par_loaded = sem("x_loaded"), sem("par_loaded")
        consts, par_ready = sem("consts"), sem("par_ready")
        sgu_par, sgu_mask = sem("sgu_par"), sem("sgu_mask")
        rel_in, rel_out, bias_in, bias_ready = (
            sem("rel_in"), sem("rel_out"), sem("bias_in"), sem("bias_ready"))
        bias_turned, bias_read = sem("bias_turned"), sem("bias_read")
        sumsq, xn_ready, xt_made, xt_hi, xt_lo = (
            sem("sumsq"), sem("xn_ready"), sem("xt_made"), sem("xt_hi"), sem("xt_lo"))
        h_ready = sem("h_ready")
        conv_v, conv_p = sem("conv_v"), sem("conv_p")
        tap_made, tap_added = sem("tap_made"), sem("tap_added")
        mean_made, centred, squared, var_made, conv_norm, conv_act, conv_y, conv_hi_s, conv_lo_s = (
            sem("mean_made"), sem("centred"), sem("squared"), sem("var_made"), sem("conv_norm"),
            sem("conv_act"), sem("conv_y"), sem("conv_hi"), sem("conv_lo"))
        vn_ready, mix_made, um_ready, um_hi, um_lo = (
            sem("vn_ready"), sem("mix_made"), sem("um_ready"), sem("um_hi"), sem("um_lo"))
        s_made, s_read, s_max, s_exp, p_ready, pt_made, pt_read, o_made, o_hi, o_lo = (
            sem("s_made"), sem("s_read"), sem("s_max"), sem("s_exp"), sem("p_ready"),
            sem("pt_made"), sem("pt_read"), sem("o_made"), sem("o_hi"), sem("o_lo"))
        mrg_ready, mrg_hi_s, mrg_lo_s = sem("mrg_ready"), sem("mrg_hi"), sem("mrg_lo")
        fh_hi_s, fh_lo_s = sem("fh_hi"), sem("fh_lo")
        wide_loaded, xg_ready, tok_hi_s, tok_lo_s, route_read = (
            sem("wide_loaded"), sem("xg_ready"), sem("tok_hi"), sem("tok_lo"), sem("route_read"))
        router_in, route_const, logits_made, gap_ready, gap_exp, chosen_ready, rank_made, flag_ready = (
            sem("router_in"), sem("route_const"), sem("logits_made"), sem("gap_ready"), sem("gap_exp"),
            sem("chosen_ready"), sem("rank_made"), sem("flag_ready"))
        pick_ready, gathered, slots_a, slots_v = (
            sem("pick_ready"), sem("gathered"), sem("slots_a"), sem("slots_v"))
        pickT_made, pickT_read = sem("pickT_made"), sem("pickT_read")
        eh_made, eh_hi_s, eh_lo_s = sem("eh_made"), sem("eh_hi"), sem("eh_lo")
        ye_hi_s, ye_lo_s, spread, spread_read = (
            sem("ye_hi"), sem("ye_lo"), sem("spread"), sem("spread_read"))
        moe_done, final_step, out_ready, out_stored = (
            sem("moe_done"), sem("final_step"), sem("out_ready"), sem("out_stored"))
        act_step, dve_step, pool_step = sem("act_step"), sem("dve_step"), sem("pool_step")

        block = ctx.enter_context(nc.Block())

        def pcol(layer, c, n=1, half=False):
            a = layer * C_LAYER + c
            return (par_half if half else par)[:, a:a + n]

        @block.sync
        def _(sp):
            def load(u, view, src, turn=None):
                if u >= RAW:
                    sp.wait_ge(lo_made, at(u - RAW + 1, turn, 12))
                dst = raw[:, u % RAW, :]
                if view > 1:
                    dst = dst.rearrange("p (k n) -> p k n", k=view)
                sp.dma_start(dst, src).then_inc(raw_loaded[u % RAW], 16)

            sp.dma_start(h[:, :, :], x.rearrange("b (i p) d -> p (b i) d", p=P)).then_inc(x_loaded, 16)

            def load_mix(layer):
                base = MIX_BASE[layer]
                w = w_in[layer].rearrange("(k p) n -> p k n", p=P)
                u = base

                def columns(c):
                    nonlocal u
                    load(u, KD, w[:, :, c:c + P])
                    u += 1

                def rows(c):
                    nonlocal u
                    for k in range(0, KD, 2):
                        load(u, 2, w[:, k:k + 2, c:c + 512])
                        u += 1

                for c in range(CG):
                    columns(CW + c * P)
                    columns(c * P)
                for c in range(4):
                    columns(1024 + c * P)
                rows(1536)
                for c in range(8):
                    columns(2048 + c * P)
                rows(3072)
                outs = [sgu_out_w, conv_out_w, attn_out_w]
                for b in range(3):
                    wo = outs[b][layer].rearrange("(k p) n -> p k n", p=P)
                    for pair in range(4):
                        for m in range(2):
                            columns(3584 + (BRANCH_GATE[b] + 2 * pair + m) * P)
                        load(u, 4, wo[:, :, pair * 256:pair * 256 + 256])
                        u += 1
                for k in range(KD):
                    load(u, 1, w_out[layer, k * P:(k + 1) * P, :])
                    u += 1
                assert u == base + MIX_UNITS

            wg = ffn_w_gate[0].rearrange("(k p) n -> p k n", p=P)
            wu = ffn_w_up[0].rearrange("(k p) n -> p k n", p=P)
            wd = ffn_w_down[0].rearrange("(f p) n -> f p n", p=P)

            def load_ffn(f, turn=None, down=True):
                u = FFN_BASE + (2 + 3 * (f - 1) if f else 0)
                c = at(f * P, turn, 4 * P)
                load(u, KD, wg[:, :, bass.ds(c, P)], turn)
                load(u + 1, KD, wu[:, :, bass.ds(c, P)], turn)
                if down:
                    src = wd[bass.ds(at(f - 1, turn, 4), 1)].rearrange("a p n -> (a p) n")
                    load(u + 2, 1, src, turn)

            def load_expert(rnd, e, first=0, end=MOE_UNITS):
                u = MOE_BASE + MOE_UNITS * NE * rnd
                g = moe_w_gate[0].rearrange("e (k p) n -> e p k n", p=P)[bass.ds(e, 1)].rearrange("a p k n -> (a p) k n")
                up = moe_w_up[0].rearrange("e (k p) n -> e p k n", p=P)[bass.ds(e, 1)].rearrange("a p k n -> (a p) k n")
                dn = moe_w_down[0].rearrange("e (f p) n -> e p f n", p=P)[bass.ds(e, 1)].rearrange("a p f n -> (a p) f n")

                start = u

                def one(view, src):
                    nonlocal u
                    if first <= u - start < end:
                        sp.wait_ge(lo_made, at(u - RAW + 1, e, MOE_UNITS))
                        dst = raw[:, u % RAW, :]
                        sp.dma_start(dst.rearrange("p (k n) -> p k n", k=view), src).then_inc(raw_loaded[u % RAW], 16)
                    u += 1

                def down(j):
                    for k in range(4):
                        one(1, dn[:, 4 * j + k:4 * j + k + 1, :])

                for j in range(NJ):
                    for w in (g, up):
                        for k in range(0, KD, 2):
                            one(2, w[:, k:k + 2, j * 512:(j + 1) * 512])
                    if j:
                        down(j - 1)
                down(NJ - 1)

            load_mix(0)
            load_ffn(0, down=False)
            with sp.Fori(0, 5) as turn:
                for f in range(1, 5):
                    load_ffn(f, turn)
            load_ffn(FT - 1)
            load(FFN_BASE + FFN_UNITS - 1, 1, wd[FT - 1])
            load_mix(1)
            with sp.Fori(0, NE) as e:
                load_expert(0, e)
            load_expert(1, 0, end=AHEAD)
            sp.wait_ge(flag_ready, 1)
            again = sp.value_load(flag[0:1, 0:1], min_val=0, max_val=1)
            with sp.If(again > 0):
                load_expert(1, 0, first=AHEAD)
                with sp.Fori(1, NE) as e:
                    load_expert(1, e)
                load_expert(2, 0, end=AHEAD)
            o = out.rearrange("b (i p) d -> (b i) p d", p=P)
            for i in range(NT):
                sp.wait_ge(out_ready, i + 1)
                sp.dma_start(o[i], xn_tok[:, i, :]).then_inc(out_stored, 16)
            sp.wait_ge(out_stored, 16 * NT)

        @block.scalar
        def _(act):
            order = Order(act, act_step)

            def split_hi(u, turn=None, stride=12):
                act.wait_ge(raw_loaded[u % RAW], at(16 * (u // RAW + 1), turn, 16 * stride // RAW))
                if u >= SPLIT or turn is not None:
                    act.wait_ge(unit_used, at(u - SPLIT + 1, turn, stride))
                act.activation(whi[:, u % SPLIT, :], raw[:, u % RAW, :], ACT.Copy).then_inc(hi_made, 1)

            def norm_sums(n):
                for i in range(NT):
                    if n == 0:
                        act.wait_ge(x_loaded, 16)
                    else:
                        act.wait_ge(h_ready, 2 * (n - 1) + i + 1)
                    act.activation(xn_tok[:, i, :], h[:, i, :], ACT.Square,
                                   accum_out=small[:, i:i + 1]).then_inc(sumsq, 1)

            def norm_hi(n, gain):
                for k in range(KD):
                    act.wait_ge(xt_made, 4 * n + k // 2 + 1)
                    act.activation(xT_hi[:, k, :], bank[4 + k // 2][:, (k % 2) * T:(k % 2 + 1) * T],
                                   ACT.Copy, scale=gain[:, k:k + 1]).then_inc(xt_hi, 1)

            def mix(layer):
                base, heads, y0 = MIX_BASE[layer], HEADS * layer, Y_USES * layer
                uses0 = A_BASE[layer] // 2

                def used(u):
                    act.wait_ge(unit_used, base + u + 1)

                def tap(k):
                    if k == 0:
                        act.wait_ge(a_read[1], uses0 + 4)
                    if k >= 3:
                        act.wait_ge(tap_added, (TAPS - 1) * layer + k - 2)
                    dst = tap_act[:, k % 2, :] if k else cacc[:, 3, :]
                    act.activation(dst, cin[:, 3, k:k + T], ACT.Copy,
                                   scale=pcol(layer, C_CONVW + TAPS * 3 + k)).then_inc(tap_made, 1)

                taps_done = 0
                for u in range(MIX_UNITS):
                    split_hi(base + u + AHEAD)
                    while u >= 8 and taps_done < min(TAPS, 3 + (u - 8) * 6 // 5):
                        tap(taps_done)
                        taps_done += 1
                    if u < 8 and u % 2 == 0:
                        c = u // 2
                        if c >= 2:
                            act.wait_ge(a_read[1], uses0 + c - 1)
                        used(u)
                        act.activation(sig[:, c % 2, :], bank[0][:, 0:T], ACT.Tanh, scale=0.5)\
                           .then_inc(a_read[0], 1)
                    elif 8 <= u < 12:
                        used(u)
                        act.activation(uT[:, u - 8, :], bank[u % 2][:, 0:T], ACT.Gelu).then_inc(a_read[u % 2], 1)
                    elif u == 15:
                        used(u)
                        for i in range(NT):
                            act.activation(v_tok[:, i, :], bank[2 + i][:, :], ACT.Gelu).then_inc(y_read[i], 1)
                    elif 16 <= u < 24:
                        used(u)
                        dst = (qT if u < 20 else kT)[:, u % 4, :]
                        act.activation(dst, bank[u % 2][:, 0:T], ACT.Copy).then_inc(a_read[u % 2], 1)
                    elif u == 27:
                        used(u)
                        for i in range(NT):
                            act.activation(v_att[:, i, :], bank[2 + i][:, :], ACT.Copy).then_inc(y_read[i], 1)
                    if 20 <= u < 24:
                        act.wait_ge(bias_turned, 4 * layer + u - 19)
                        act.activation(bias_t[:, 2 * (u - 20):2 * (u - 20) + 2, :],
                                       bank[4 + u % 2][:, :].rearrange("p (a t) -> p a t", a=2),
                                       ACT.Copy).then_inc(bias_read, 1)
                    if u == 19:
                        act.wait_ge(um_ready, layer + 1)
                        act.activation(sgu_hi, um, ACT.Copy).then_inc(um_hi, 1)
                    for b in range(3):
                        g = u - BRANCH_UNIT[b]
                        if 0 <= g < 12 and g % 3 < 2:
                            m, yi = 2 * (g // 3) + g % 3, 4 * b + g // 3
                            parity = m % 2
                            if yi >= 2:
                                act.wait_ge(y_read[yi % 2], y0 + 3 + yi // 2)
                            used(u)
                            act.activation(gate_t[:, yi % 2, m % 2, :], bank[parity][:, 0:T], ACT.Tanh,
                                           scale=0.5, bias=pcol(layer, C_GATEB + BRANCH_GATE[b] + m, half=True))\
                               .then_inc(a_read[parity], 1)
                    if u == 35:
                        act.wait_ge(centred, layer + 1)
                        act.activation(csq, cacc[:, :, :], ACT.Square).then_inc(squared, 1)
                    if u == 37:
                        act.wait_ge(conv_norm, layer + 1)
                        for c in range(CG):
                            order.mark(act.activation(csq[:, c, :], cacc[:, c, :], ACT.Tanh,
                                                      scale=pcol(layer, C_LNG + c, half=True),
                                                      bias=pcol(layer, C_LNB + c, half=True)))
                        act.wait_ge(act_step, order.value())
                        for c in range(CG):
                            act.activation(cacc[:, c, :], cacc[:, c, :], ACT.Identity,
                                           scale=pcol(layer, C_LNG + c), bias=pcol(layer, C_LNB + c))\
                               .then_inc(conv_act, 1)
                    if u == 39:
                        act.wait_ge(conv_y, layer + 1)
                        act.activation(conv_hi, cacc[:, :, :], ACT.Copy, scale=0.5).then_inc(conv_hi_s, 1)
                    for hd in range(HEADS):
                        s = SLOT_OF_HEAD[hd]
                        if u == s:
                            act.wait_ge(s_max, heads + hd + 1)
                            for q, (a, b) in enumerate(((0, 256), (256, 384))):
                                act.activation(S[:, hd % 2, a:b], S[:, hd % 2, a:b], ACT.Exp,
                                               bias=small[:, 8 + 2 * (hd % 2) + q:9 + 2 * (hd % 2) + q],
                                               accum_out=small[:, 12 + 2 * (hd % 2) + q:13 + 2 * (hd % 2) + q])\
                                   .then_inc(s_exp, 1)
                        if u == s + 2:
                            act.wait_ge(pt_made, heads + hd + 1)
                            if hd >= 2:
                                act.wait_ge(o_made, heads + hd - 1)
                            act.activation(pT[:, hd % 2, :], bank[6][:, 0:384], ACT.Copy).then_inc(pt_read, 1)
                        if u == s + 3 and hd % 2:
                            act.wait_ge(o_made, heads + hd + 1)
                            act.activation(attn_hi[:, hd // 2, :], bank[7][:, 0:T], ACT.Copy).then_inc(o_hi, 1)
                    if u >= BRANCH_UNIT[2] and (u - BRANCH_UNIT[2]) % 3 == 2 and u < 64:
                        pair = (u - BRANCH_UNIT[2]) // 3
                        act.wait_ge(mrg_ready, 4 * layer + pair + 1)
                        act.activation(mrg_hi[:, 2 * pair:2 * pair + 2, :], merged[:, 2 * pair:2 * pair + 2, :],
                                       ACT.Copy, scale=0.5).then_inc(mrg_hi_s, 1)

            def ffn_silu(f, turn=None):
                u = FFN_BASE + (2 + 3 * (f - 1) if f else 0)
                act.wait_ge(unit_used, at(u + 1, turn, 12))
                if f >= 2 or turn is not None:
                    act.wait_ge(a_read[1], at(FFN_A_BASE // 2 + f - 1, turn, 4))
                act.activation(f_sl[:, f % 2, :], bank[0][:, 0:T], ACT.Silu).then_inc(a_read[0], 1)

            def ffn_hi(f, turn=None):
                act.wait_ge(a_read[1], at(FFN_A_BASE // 2 + f + 1, turn, 4))
                if f >= 2 or turn is not None:
                    act.wait_ge(unit_used, at(FFN_BASE + 2 + 3 * (f - 2) + 3, turn, 12))
                act.activation(fh_hi[:, f % 2, :], f_h[:, f % 2, :], ACT.Copy).then_inc(fh_hi_s, 1)

            def ffn_step(f, turn=None):
                u = FFN_BASE + 2 + 3 * (f - 1)
                split_hi(u + AHEAD, turn)
                split_hi(u + 1 + AHEAD, turn)
                ffn_silu(f, turn)
                split_hi(u + 2 + AHEAD, turn)
                ffn_hi(f, turn)

            def expert(rnd, e):
                u0 = MOE_BASE + MOE_UNITS * NE * rnd
                for k in range(MOE_UNITS):
                    split_hi(u0 + k + AHEAD, e, MOE_UNITS)
                    j, q = (0, k) if k < 8 else ((k - 8) // 12 + 1, (k - 8) % 12)
                    if j < NJ and q == 1 and j:
                        expert_hi(rnd, e, j - 1)
                    if j < NJ and q == 3:
                        c = NJ * (NE * rnd) + j
                        act.wait_ge(unit_used, at(u0 + k + 1, e, MOE_UNITS))
                        act.wait_ge(a_read[1], at(MOE_A_USES + c, e, NJ))
                        act.activation(e_sl, bank[0][:, :], ACT.Silu).then_inc(a_read[0], 1)
                    if j == 1 and q == 8:
                        act.wait_ge(pickT_made, at(NE * rnd + 1, e, 1))
                        act.activation(pickT, bank[7][:, 0:T], ACT.Copy).then_inc(pickT_read, 1)
                    if j == NJ - 1 and q == 7:
                        gather_read(9 * rnd + 1, e, (0,))
                        expert_hi(rnd, e, NJ - 1)
                        gather_read(9 * rnd + 1, e, (2,))
                act.wait_ge(unit_used, at(u0 + MOE_UNITS, e, MOE_UNITS))
                for n in range(2):
                    act.activation(ye_hi[:, n * 512:(n + 1) * 512], bank[4 + n][:, :], ACT.Copy).then_inc(ye_hi_s, 1)

            def expert_hi(rnd, e, j):
                act.wait_ge(eh_made, at(NJ * NE * rnd + j + 1, e, NJ))
                act.activation(eh_hi, bank[2][:, :], ACT.Copy).then_inc(eh_hi_s, 1)

            def gather_read(n, e=None, rounds=(0, 2)):
                for r in rounds:
                    act.wait_ge(gathered, at(4 * n + r + 1, e, 4))
                    act.activation(slot_parts[r // 2][:, 0:4, :], bank[3][:, :], ACT.Copy).then_inc(slots_a, 1)

            norm_sums(0)
            for u in range(AHEAD):
                split_hi(u)
            act.wait_ge(par_loaded, 16)
            norm_hi(0, pcol(0, C_MIXG, 8))
            act.wait_ge(par_ready, 1)
            mix(0)
            norm_sums(1)
            norm_hi(1, pcol(0, C_FFNG, 8))
            split_hi(FFN_BASE + AHEAD)
            split_hi(FFN_BASE + 1 + AHEAD)
            ffn_silu(0)
            ffn_hi(0)
            with act.Fori(0, 5) as turn:
                for f in range(1, 5):
                    ffn_step(f, turn)
            ffn_step(FT - 1)
            split_hi(FFN_BASE + FFN_UNITS - 1 + AHEAD)
            norm_sums(2)
            norm_hi(2, pcol(1, C_MIXG, 8))
            mix(1)
            norm_sums(3)
            for i in range(NT):
                act.wait_ge(xg_ready, i + 1)
                act.activation(tok_hi[:, i, :], xn_tok[:, i, :], ACT.Copy).then_inc(tok_hi_s, 1)
            for k in range(4):
                act.wait_ge(xt_made, 4 * 3 + k + 1)
                act.activation(routeT[:, 2 * k:2 * k + 2, :], bank[4 + k][:, :].rearrange("p (a t) -> p a t", a=2),
                               ACT.Copy).then_inc(route_read, 1)
            act.wait_ge(gap_ready, 2)
            act.activation(small[:, 24:26], small[:, 20:22], ACT.Exp).then_inc(gap_exp, 1)
            gather_read(0)
            with act.Fori(0, NE) as e:
                expert(0, e)
            act.wait_ge(flag_ready, 1)
            again = act.value_load(flag[0:1, 0:1], min_val=0, max_val=1)
            with act.If(again > 0):
                gather_read(9)
                with act.Fori(0, NE) as e:
                    expert(1, e)
            for i in range(NT):
                act.wait_ge(moe_done, 1)
                act.activation(xn_tok[:, i, :], h[:, i, :], ACT.Square,
                               accum_out=small[:, i:i + 1]).then_inc(sumsq, 1)

        @block.vector
        def _(dve):
            order = Order(dve, dve_step)

            def split_lo(u, turn=None, stride=12):
                dve.wait_ge(hi_made, at(u + 1, turn, stride))
                dve.tensor_tensor(wlo[:, u % SPLIT, :], raw[:, u % RAW, :], whi[:, u % SPLIT, :],
                                  ALU.subtract).then_inc(lo_made, 1)

            def rsqrt(v, y, t):
                vi, yi, ti = v.bitcast(I32), y.bitcast(I32), t.bitcast(I32)
                order.link(dve.tensor_scalar(ti, vi, 1, None, ALU.logical_shift_right))
                order.link(dve.tensor_scalar(yi, ti, -1.0, RSQRT_SEED, ALU.mult, ALU.add))
                for _ in range(3):
                    order.link(dve.tensor_tensor(t, y, y, ALU.mult))
                    order.link(dve.scalar_tensor_tensor(t, t, -0.5, v, ALU.mult, ALU.mult))
                    order.link(dve.scalar_tensor_tensor(y, t, 1.5, y, ALU.add, ALU.mult))

            def norm_scale(n):
                dve.wait_ge(sumsq, 2 * n + 2)
                order.link(dve.tensor_scalar(small[:, 2:4], small[:, 0:2], 1.0 / D, EPS, ALU.mult, ALU.add))
                rsqrt(small[:, 2:4], small[:, 4:6], small[:, 6:8])
                for i in range(NT):
                    ins = dve.tensor_scalar(xn_tok[:, i, :], h[:, i, :], small[:, 4 + i:5 + i], None, ALU.mult)
                    if n < 3:
                        ins.then_inc(xn_ready, 1)
                    else:
                        order.link(ins)

            def norm_lo(n, gain):
                for k in range(KD):
                    dve.wait_ge(xt_hi, 8 * n + 2 * (k // 2) + 2)
                    dve.scalar_tensor_tensor(xT_lo[:, k, :], bank[4 + k // 2][:, (k % 2) * T:(k % 2 + 1) * T],
                                             gain[:, k:k + 1], xT_hi[:, k, :], ALU.mult, ALU.subtract)\
                       .then_inc(xt_lo, 1)

            def add_to_h():
                for i in range(NT):
                    for n in range(2):
                        part = h[:, i, n * 512:(n + 1) * 512]
                        ins = dve.tensor_tensor(part, bank[4 + 2 * i + n][:, :], part, ALU.add)
                        if n:
                            ins.then_inc(h_ready, 1)
                        else:
                            order.mark(ins)

            def mix(layer):
                base, heads, y0 = MIX_BASE[layer], HEADS * layer, Y_USES * layer
                uses0 = A_BASE[layer] // 2

                def used(u):
                    dve.wait_ge(unit_used, base + u + 1)

                def tap(n):
                    k, c = divmod(n, 2)
                    if n == 0:
                        dve.wait_ge(a_read[1], uses0 + 2)
                    dve.wait_ge(dve_step, order.value(0 if k == TAPS else 1))
                    if k < TAPS:
                        src, w = cin[:, c, k:k + T], pcol(layer, C_CONVW + TAPS * c + k)
                    if k == 0:
                        order.mark(dve.tensor_scalar(cacc[:, c, :], src, w, None, ALU.mult))
                    elif k < TAPS:
                        order.mark(dve.scalar_tensor_tensor(cacc[:, c, :], src, w, cacc[:, c, :],
                                                            ALU.mult, ALU.add))
                    else:
                        dve.tensor_scalar(cacc[:, c, :], cacc[:, c, :], 0.5, pcol(layer, C_CONVB + c),
                                          ALU.mult, ALU.add).then_inc(conv_v, 1)

                taps_done = 0
                for u in range(MIX_UNITS):
                    split_lo(base + u + AHEAD)
                    if u < 8 and u % 2:
                        c = u // 2
                        dve.wait_ge(a_read[0], uses0 + c + 1)
                        used(u)
                        dve.scalar_tensor_tensor(cin[:, c, TAPS - 1:], sig[:, c % 2, :], 1.0, bank[1][:, 0:T],
                                                 ALU.add, ALU.mult).then_inc(a_read[1], 1)
                    if u >= 4 and taps_done < 2 * (TAPS + 1):
                        for _ in range(min(3, 2 * (TAPS + 1) - taps_done)):
                            tap(taps_done)
                            taps_done += 1
                    if u == 15:
                        for i in range(NT):
                            dve.wait_ge(y_read[i], y0 + 1)
                            order.link(dve.bn_stats(small[:, 48:54], v_tok[:, i, :]))
                            order.link(dve.bn_aggr(small[:, 28 + 2 * i:30 + 2 * i], small[:, 48:54]))
                        var = small[:, 28:32].rearrange("p (i s) -> p i s", s=2)[:, :, 1]
                        order.link(dve.tensor_scalar(small[:, 32:34], var, EPS, None, ALU.add))
                        rsqrt(small[:, 32:34], small[:, 34:36], small[:, 36:38])
                        dve.wait_ge(sgu_par, 64 * (layer + 1))
                        for i in range(NT):
                            v = v_tok[:, i, :]
                            order.link(dve.tensor_scalar(v, v, small[:, 28 + 2 * i:29 + 2 * i],
                                                         small[:, 34 + i:35 + i], ALU.subtract, ALU.mult))
                            order.link(dve.tensor_tensor(v, v, ln_gb[:, 0, :], ALU.mult))
                            dve.tensor_tensor(v, v, ln_gb[:, 1, :], ALU.add).then_inc(vn_ready, 1)
                    if u == 18:
                        dve.wait_ge(mix_made, layer + 1)
                        for g in range(4):
                            src = bank[2 + g // 2][:, (g % 2) * T:(g % 2 + 1) * T].rearrange("p (n t) -> p n t", n=2)
                            dst = um[:, g, :].rearrange("p (n t) -> p n t", n=2)
                            ins = dve.tensor_tensor(dst, src, bs_b[:, g:g + 1, :].to_broadcast([P, 2, P]), ALU.add)
                            if g % 2:
                                ins.then_inc(y_read[g // 2], 1)
                            else:
                                order.mark(ins)
                        dve.wait_ge(y_read[1], y0 + 2)
                        dve.tensor_tensor(um, um, uT[:, :, :], ALU.mult).then_inc(um_ready, 1)
                    if u == 20:
                        dve.wait_ge(um_hi, layer + 1)
                        dve.tensor_tensor(sgu_lo, um, sgu_hi, ALU.subtract).then_inc(um_lo, 1)
                    if u == 34:
                        dve.wait_ge(mean_made, layer + 1)
                        dve.tensor_tensor(cacc[:, :, :], cacc[:, :, :],
                                          bank[5][:, 0:T].unsqueeze(1).to_broadcast([P, CG, T]),
                                          ALU.subtract).then_inc(centred, 1)
                    if u == 36:
                        dve.wait_ge(var_made, layer + 1)
                        order.link(dve.tensor_scalar(stat[:, 0, :], bank[5][:, T:2 * T], EPS, None, ALU.add))
                        rsqrt(stat[:, 0, :], stat[:, 1, :], stat[:, 2, :])
                        dve.tensor_tensor(cacc[:, :, :], cacc[:, :, :],
                                          stat[:, 1:2, :].to_broadcast([P, CG, T]), ALU.mult).then_inc(conv_norm, 1)
                    if u == 38:
                        dve.wait_ge(conv_act, CG * (layer + 1))
                        dve.scalar_tensor_tensor(cacc[:, :, :], csq, 1.0, cacc[:, :, :], ALU.add, ALU.mult)\
                           .then_inc(conv_y, 1)
                    if u == 40:
                        dve.wait_ge(conv_hi_s, layer + 1)
                        dve.scalar_tensor_tensor(conv_lo, cacc[:, :, :], 0.5, conv_hi, ALU.mult, ALU.subtract)\
                           .then_inc(conv_lo_s, 1)
                    for hd in range(HEADS):
                        s, two, par2 = SLOT_OF_HEAD[hd], hd % 2, 2 * (hd % 2)
                        if u == s:
                            dve.wait_ge(s_made, heads + hd + 1)
                            dve.wait_ge(bias_read, 4 * (layer + 1))
                            if hd >= 2:
                                dve.wait_ge(pt_made, heads + hd - 1)
                            order.mark(dve.scalar_tensor_tensor(S[:, two, 0:256], bank[4][:, 0:256], HD ** -0.5,
                                                                bias_t[:, hd, :], ALU.mult, ALU.add))
                            dve.scalar_tensor_tensor(S[:, two, 256:384], bank[4][:, 256:384], HD ** -0.5,
                                                     bias_t[:, hd, P:], ALU.mult, ALU.add).then_inc(s_read, 1)
                            dve.wait_ge(s_read, heads + hd + 1)
                            for q, (a, b) in enumerate(((0, 256), (256, 384))):
                                ins = dve.tensor_reduce(small[:, 8 + par2 + q:9 + par2 + q], S[:, two, a:b],
                                                        AX.X, ALU.max, negate=True)
                                if q:
                                    ins.then_inc(s_max, 1)
                                else:
                                    order.mark(ins)
                        if u == s + 1:
                            dve.wait_ge(s_exp, 2 * (heads + hd + 1))
                            order.link(dve.reciprocal(small[:, 16 + par2:18 + par2], small[:, 12 + par2:14 + par2]))
                            for q, (a, b) in enumerate(((0, 256), (256, 384))):
                                dve.tensor_scalar(S[:, two, a:b], S[:, two, a:b],
                                                  small[:, 16 + par2 + q:17 + par2 + q], None, ALU.mult)\
                                   .then_inc(p_ready, 1)
                        if u == s + 4 and two:
                            dve.wait_ge(o_hi, (heads + hd + 1) // 2)
                            dve.tensor_tensor(attn_lo[:, hd // 2, :], bank[7][:, 0:T], attn_hi[:, hd // 2, :],
                                              ALU.subtract).then_inc(o_lo, 1)
                    for b in range(3):
                        g = u - BRANCH_UNIT[b]
                        if 0 <= g < 12 and g % 3 == 2:
                            pair, yi = g // 3, 4 * b + g // 3
                            a_uses = uses0 + 10 + 4 * b + pair + 1
                            dve.wait_ge(a_read[0], a_uses)
                            dve.wait_ge(a_read[1], a_uses)
                            used(u)
                            y = bank[2 + yi % 2][:, :].rearrange("p (m t) -> p m t", m=2)
                            dst = merged[:, 2 * pair:2 * pair + 2, :]
                            tmp = dst if b == 0 else mtmp
                            if b == 2 and pair:
                                dve.wait_ge(mrg_ready, 4 * layer + pair)
                            dve.scalar_tensor_tensor(tmp, gate_t[:, yi % 2, :, :], 1.0, y, ALU.add, ALU.mult)\
                               .then_inc(y_read[yi % 2], 1)
                            if b:
                                dve.wait_ge(y_read[yi % 2], y0 + 3 + yi // 2 + 1)
                                ins = dve.tensor_tensor(dst, dst, tmp, ALU.add)
                                if b == 2:
                                    ins.then_inc(mrg_ready, 1)
                                else:
                                    order.link(ins)
                    if u >= BRANCH_UNIT[2] + 3 and (u - BRANCH_UNIT[2]) % 3 == 0 and u <= 64:
                        pair = (u - BRANCH_UNIT[2]) // 3 - 1
                        merged_lo(layer, pair)
                used(MIX_UNITS - 1)
                add_to_h()

            def merged_lo(layer, pair):
                dve.wait_ge(mrg_hi_s, 4 * layer + pair + 1)
                dve.scalar_tensor_tensor(mrg_lo[:, 2 * pair:2 * pair + 2, :], merged[:, 2 * pair:2 * pair + 2, :],
                                         0.5, mrg_hi[:, 2 * pair:2 * pair + 2, :], ALU.mult, ALU.subtract)\
                   .then_inc(mrg_lo_s, 1)

            def ffn_mul(f, turn=None):
                u = FFN_BASE + (2 + 3 * (f - 1) if f else 0) + 1
                dve.wait_ge(unit_used, at(u + 1, turn, 12))
                dve.wait_ge(a_read[0], at(FFN_A_BASE // 2 + f + 1, turn, 4))
                dve.tensor_tensor(f_h[:, f % 2, :], f_sl[:, f % 2, :], bank[1][:, 0:T], ALU.mult)\
                   .then_inc(a_read[1], 1)

            def ffn_lo(f, turn=None):
                dve.wait_ge(fh_hi_s, at(f + 1, turn, 4))
                dve.tensor_tensor(fh_lo[:, f % 2, :], f_h[:, f % 2, :], fh_hi[:, f % 2, :], ALU.subtract)\
                   .then_inc(fh_lo_s, 1)

            def ffn_step(f, turn=None):
                u = FFN_BASE + 2 + 3 * (f - 1)
                split_lo(u + AHEAD, turn)
                split_lo(u + 1 + AHEAD, turn)
                ffn_mul(f, turn)
                split_lo(u + 2 + AHEAD, turn)
                ffn_lo(f, turn)

            def build_pick(n, e=None):
                if e is not None:
                    dve.wait_ge(pickT_made, at(n - n // 9, e, 1))
                elif n == 0:
                    dve.wait_ge(pickT_read, 1)
                for i in range(NT):
                    c = bass.ds(at(0 if e is None else 1, e, 1), 1)
                    ins = dve.tensor_scalar(pick[:, i, :], iota, slot[:, i, c], chosen[:, i, c],
                                            ALU.is_equal, ALU.mult)
                    ins.then_inc(pick_ready, 1)

            def gather_read(n, e=None, rounds=(1, 3)):
                for r in rounds:
                    dve.wait_ge(gathered, at(4 * n + r + 1, e, 4))
                    dve.tensor_copy(slot_parts[r // 2][:, 4:8, :],
                                    bank[6][:, :].rearrange("p (k s) -> p k s", k=4)).then_inc(slots_v, 1)

            def expert_lo(rnd, e, j):
                dve.wait_ge(eh_hi_s, at(NJ * NE * rnd + j + 1, e, NJ))
                dve.tensor_tensor(eh_lo, bank[2][:, :].rearrange("p (k s) -> p k s", k=4), eh_hi,
                                  ALU.subtract).then_inc(eh_lo_s, 1)

            def spread_add(n, q, e=None):
                i, half = divmod(q, 2)
                dve.wait_ge(spread, at(4 * n + q + 1, e, 4))
                part = h[:, i, half * 512:(half + 1) * 512]
                c = bass.ds(at(0, e, 1), 1) if e is not None else slice(NE, NE + 1)
                dve.scalar_tensor_tensor(part, bank[6 + q % 2][:, :], weight[:, i, c], part,
                                         ALU.mult, ALU.add).then_inc(spread_read, 1)

            def expert(rnd, e):
                u0 = MOE_BASE + MOE_UNITS * NE * rnd
                for k in range(MOE_UNITS):
                    split_lo(u0 + k + AHEAD, e, MOE_UNITS)
                    j, q = (0, k) if k < 8 else ((k - 8) // 12 + 1, (k - 8) % 12)
                    if j == 0 and q in (4, 5):
                        spread_add(9 * rnd, q - 4, e)
                    if j == 1 and q in (0, 1):
                        spread_add(9 * rnd, q + 2, e)
                    if 0 < j < NJ and q == 2:
                        expert_lo(rnd, e, j - 1)
                    if j < NJ and q == 7:
                        c = NJ * NE * rnd + j
                        dve.wait_ge(unit_used, at(u0 + k + 1, e, MOE_UNITS))
                        dve.wait_ge(a_read[0], at(MOE_A_USES + c + 1, e, NJ))
                        dve.tensor_tensor(e_h, e_sl, bank[1][:, :], ALU.mult).then_inc(a_read[1], 1)
                    if j == 2 and q == 0:
                        build_pick(9 * rnd + 1, e)
                    if j == NJ - 1 and q == 7:
                        gather_read(9 * rnd + 1, e, (1,))
                        expert_lo(rnd, e, NJ - 1)
                        gather_read(9 * rnd + 1, e, (3,))
                for n in range(2):
                    dve.wait_ge(ye_hi_s, at(2 * NE * rnd + n + 1, e, 2))
                    part = slice(n * 512, (n + 1) * 512)
                    dve.tensor_tensor(ye_lo[:, part], bank[4 + n][:, :], ye_hi[:, part], ALU.subtract)\
                       .then_inc(ye_lo_s, 1)

            dve.wait_ge(par_loaded, 16)
            dve.tensor_scalar(par_half[:, :], par[:, :], 0.5, None, ALU.mult).then_inc(par_ready, 1)
            order.mark(dve.memset(cin[:, :, 0:TAPS - 1], 0.0))
            norm_scale(0)
            for u in range(AHEAD):
                split_lo(u)
            norm_lo(0, pcol(0, C_MIXG, 8))
            mix(0)
            norm_scale(1)
            norm_lo(1, pcol(0, C_FFNG, 8))
            split_lo(FFN_BASE + AHEAD)
            split_lo(FFN_BASE + 1 + AHEAD)
            ffn_mul(0)
            ffn_lo(0)
            with dve.Fori(0, 5) as turn:
                for f in range(1, 5):
                    ffn_step(f, turn)
            ffn_step(FT - 1)
            split_lo(FFN_BASE + FFN_UNITS - 1 + AHEAD)
            dve.wait_ge(unit_used, FFN_BASE + FFN_UNITS)
            add_to_h()
            norm_scale(2)
            norm_lo(2, pcol(1, C_MIXG, 8))
            mix(1)

            norm_scale(3)
            dve.wait_ge(wide_loaded, 32)
            for i in range(NT):
                dve.tensor_tensor(xn_tok[:, i, :], xn_tok[:, i, :], g_ffn_b, ALU.mult).then_inc(xg_ready, 1)
            order.mark(dve.memset(chosen[:, :, :], 0.0))
            order.mark(dve.memset(weight[:, :, :], 0.0))
            order.mark(dve.memset(rank[:, :, :], 0.0))
            dve.memset(br_ab[:, 2048:4096].bitcast(F32), 0.0).then_inc(ye_lo_s, 1)
            dve.memset(pickT.bitcast(F32), 0.0).then_inc(pickT_read, 1)
            for i in range(NT):
                dve.wait_ge(tok_hi_s, i + 1)
                dve.tensor_tensor(tok_lo[:, i, :], xn_tok[:, i, :], tok_hi[:, i, :], ALU.subtract)\
                   .then_inc(tok_lo_s, 1)
            dve.wait_ge(route_const, 2)
            dve.wait_ge(logits_made, 1)
            order.link(dve.tensor_copy(logit[:, :, :], bank[3][:, 0:16].rearrange("p (i e) -> p i e", i=2)))
            for i in range(NT):
                order.link(dve.max(top[:, i, :], logit[:, i, :]))
                order.link(dve.max_index(topi[:, i, :], top[:, i, :], logit[:, i, :]))
                dve.tensor_tensor(small[:, 20 + i:21 + i], top[:, i, 1:2], top[:, i, 0:1], ALU.subtract)\
                   .then_inc(gap_ready, 1)
            dve.wait_ge(gap_ready, 2)
            order.link(dve.tensor_copy(top[:, :, :], topi[:, :, :]))
            dve.wait_ge(gap_exp, 1)
            order.link(dve.tensor_scalar(small[:, 26:28], small[:, 24:26], 1.0, None, ALU.add))
            order.link(dve.reciprocal(small[:, 38:40], small[:, 26:28]))
            order.link(dve.tensor_tensor(small[:, 42:44], small[:, 24:26], small[:, 38:40], ALU.mult))
            for i in range(NT):
                for r in range(2):
                    order.link(dve.tensor_scalar(sel[:, r, :], iota[:, 0:NE], top[:, i, r:r + 1], None, ALU.is_equal))
                dve.tensor_tensor(chosen[:, i, 0:NE], sel[:, 0, :], sel[:, 1, :], ALU.add).then_inc(chosen_ready, 1)
                order.link(dve.tensor_scalar(sel[:, 1, :], sel[:, 1, :], small[:, 42 + i:43 + i], None, ALU.mult))
                order.link(dve.scalar_tensor_tensor(weight[:, i, 1:NE + 1], sel[:, 0, :], small[:, 38 + i:39 + i],
                                                    sel[:, 1, :], ALU.mult, ALU.add))
            dve.wait_ge(rank_made, 1)
            order.link(dve.tensor_copy(rank[:, :, 0:NE], bank[3][:, 16:32].rearrange("p (i e) -> p i e", i=2)))
            order.link(dve.tensor_reduce(small[:, 44:45], bank[3][:, 32:40], AX.X, ALU.max))
            order.link(dve.tensor_scalar(small[:, 45:46], small[:, 44:45], float(P), None, ALU.is_gt))
            dve.tensor_copy(flag[:, :], small[:, 45:46]).then_inc(flag_ready, 1)

            def experts(rnd):
                order.link(dve.tensor_scalar(slot[:, :, :], rank[:, :, :], float(-P * rnd), None, ALU.add))
                build_pick(9 * rnd)
                gather_read(9 * rnd)
                with dve.Fori(0, NE) as e:
                    expert(rnd, e)
                for q in range(4):
                    spread_add(9 * rnd + NE, q)

            experts(0)
            dve.wait_ge(flag_ready, 1)
            again = dve.value_load(flag[0:1, 0:1], min_val=0, max_val=1)
            with dve.If(again > 0):
                experts(1)
            dve.memset(small[:, 46:47], 0.0).then_inc(moe_done, 1)
            dve.wait_ge(sumsq, 2 * 4 + 2)
            v, y, t = small[:, 2:4], small[:, 4:6], small[:, 6:8]
            vi, yi, ti = v.bitcast(I32), y.bitcast(I32), t.bitcast(I32)
            last = Order(dve, final_step)
            last.link(dve.tensor_scalar(v, small[:, 0:2], 1.0 / D, EPS, ALU.mult, ALU.add))
            last.link(dve.tensor_scalar(ti, vi, 1, None, ALU.logical_shift_right))
            last.link(dve.tensor_scalar(yi, ti, -1.0, RSQRT_SEED, ALU.mult, ALU.add))
            for _ in range(3):
                last.link(dve.tensor_tensor(t, y, y, ALU.mult))
                last.link(dve.scalar_tensor_tensor(t, t, -0.5, v, ALU.mult, ALU.mult))
                last.link(dve.scalar_tensor_tensor(y, t, 1.5, y, ALU.add, ALU.mult))
            for i in range(NT):
                dve.scalar_tensor_tensor(xn_tok[:, i, :], h[:, i, :], small[:, 4 + i:5 + i], g_fin_b,
                                         ALU.mult, ALU.mult).then_inc(out_ready, 1)

        @block.tensor
        def _(pe):
            def unit(u, view, turn=None, stride=12):
                pe.wait_ge(lo_made, at(u + 1, turn, stride))
                return [w[:, u % SPLIT, :].rearrange("p (k n) -> p k n", k=view) for w in (whi, wlo)]

            def product(out_ap, a, b, first, last):
                pe.matmul(out_ap, a[0], b[0], start=first, stop=False)
                pe.matmul(out_ap, a[0], b[1], start=False, stop=False)
                return pe.matmul(out_ap, a[1], b[0], start=False, stop=last)

            def turned(out_ap, w, c, rhs, k_tiles):
                for k in range(k_tiles):
                    ins = product(out_ap, [w[0][:, k, c:c + P], w[1][:, k, c:c + P]],
                                  [rhs[0][:, k, :], rhs[1][:, k, :]], k == 0, k == k_tiles - 1)
                return ins

            def norm_turn(n):
                for i in range(NT):
                    if n < 3:
                        pe.wait_ge(xn_ready, 2 * n + i + 1)
                    else:
                        pe.wait_ge(xg_ready, i + 1)
                    for k in range(KD):
                        c = (k % 2) * T + i * P
                        ins = pe.transpose(bank[4 + k // 2][:, c:c + P], xn_tok[:, i, k * P:(k + 1) * P], ident[:, :])
                        if i and k % 2:
                            ins.then_inc(xt_made, 1)

            def mix(layer):
                base, heads, y0 = MIX_BASE[layer], HEADS * layer, Y_USES * layer
                uses0 = A_BASE[layer] // 2
                norm = 2 * layer
                xs = [xT_hi, xT_lo]
                a_index = 0

                def a_unit(u):
                    nonlocal a_index
                    b = a_index % 2
                    w = unit(base + u, KD)
                    if uses0 + a_index // 2:
                        pe.wait_ge(a_read[b], uses0 + a_index // 2)
                    if a_index == 0:
                        for k in range(KD):
                            pe.wait_ge(xt_lo, 8 * norm + k + 1)
                            ins = product(bank[b][:, 0:T], [w[0][:, k, :], w[1][:, k, :]],
                                          [xT_hi[:, k, :], xT_lo[:, k, :]], k == 0, k == KD - 1)
                    else:
                        ins = turned(bank[b][:, 0:T], w, 0, xs, KD)
                    ins.then_inc(unit_used, 1)
                    a_index += 1

                def v_units(u, use):
                    if y0 + use:
                        for i in range(NT):
                            pe.wait_ge(y_read[i], y0 + use)
                    for n in range(4):
                        w = unit(base + u + n, 2)
                        for i in range(NT):
                            for k in range(2):
                                kk = 2 * n + k
                                t = slice(i * P, (i + 1) * P)
                                ins = product(bank[2 + i][:, :], [xT_hi[:, kk, t], xT_lo[:, kk, t]],
                                              [w[0][:, k, :], w[1][:, k, :]], kk == 0, kk == KD - 1)
                        ins.then_inc(unit_used, 1)
                        extras(u + n)

                def y_unit(u, b, pair):
                    yi = 4 * b + pair
                    w = unit(base + u, 4)
                    pe.wait_ge([um_lo, conv_lo_s, o_lo][b], [layer + 1, layer + 1, 4 * layer + 4][b])
                    pe.wait_ge(y_read[yi % 2], y0 + 3 + yi // 2)
                    for m in range(2):
                        ins = turned(bank[2 + yi % 2][:, m * T:(m + 1) * T], w, m * P, branch_parts[b], 4)
                    ins.then_inc(unit_used, 1)

                def sgu_mix():
                    pe.wait_ge(vn_ready, 2 * layer + 2)
                    pe.wait_ge(sgu_mask, layer + 1)
                    for i in range(NT):
                        pe.wait_ge(y_read[i], y0 + 1)
                    for g in range(4):
                        for n in range(NT):
                            c = (g % 2) * T + n * P
                            ins = pe.matmul(bank[2 + g // 2][:, c:c + P], v_tok[:, n, g * P:(g + 1) * P],
                                            wsT[:, g, :], start=True, stop=True)
                    ins.then_inc(mix_made, 1)

                def scores(hd):
                    r, i = slice(64 * (hd % 2), 64 * (hd % 2) + 64), hd // 2
                    if hd == 0:
                        pe.wait_ge(bias_read, 4 * (layer + 1))
                        pe.wait_ge(a_read[0], uses0 + 10)
                        pe.wait_ge(a_read[1], uses0 + 10)
                    if heads + hd:
                        pe.wait_ge(s_read, heads + hd)
                    pe.matmul(bank[4][:, 0:256], qT[r, i, P:T], kT[r, i, :], start=True, stop=True)
                    pe.matmul(bank[4][:, 256:384], qT[r, i, 0:P], kT[r, i, 0:P], start=True, stop=True)\
                      .then_inc(s_made, 1)

                def turn_p(hd):
                    pe.wait_ge(p_ready, 2 * (heads + hd + 1))
                    if heads + hd:
                        pe.wait_ge(pt_read, heads + hd)
                    for n, c in enumerate((256, 0, 128)):
                        ins = pe.transpose(bank[6][:, n * P:(n + 1) * P], S[:, hd % 2, c:c + P], ident[:, :])
                    ins.then_inc(pt_made, 1)

                def head_out(hd):
                    r = slice(64 * (hd % 2), 64 * (hd % 2) + 64)
                    pe.wait_ge(pt_read, heads + hd + 1)
                    pe.wait_ge(y_read[1], y0 + 3)
                    if heads + hd > 1:
                        pe.wait_ge(o_lo, (heads + hd) // 2)
                    c = slice(hd * HD, (hd + 1) * HD)
                    pe.matmul(bank[7][r, 0:T], v_att[:, 0, c], pT[:, hd % 2, 0:T], start=True, stop=False)
                    pe.matmul(bank[7][r, P:T], v_att[:, 1, c], pT[:, hd % 2, T:384], start=False, stop=True)\
                      .then_inc(o_made, 1)

                def channel_mean(src, c0):
                    for c in range(CG):
                        ins = pe.matmul(bank[5][:, c0:c0 + T], ones[:, :], src[:, c, :], start=c == 0, stop=c == 3)
                    return ins

                def turn_bias(r):
                    pe.wait_ge(bias_ready, layer + 1)
                    if r >= 2:
                        pe.wait_ge(bias_read, 4 * layer + r - 1)
                    pe.matmul(bank[4 + r % 2][:, :], anti[:, :], bias_t[:, 2 * r:2 * r + 2, :],
                              start=True, stop=True).then_inc(bias_turned, 1)

                def extras(u):
                    if u == 18:
                        sgu_mix()
                    if 20 <= u < 24:
                        turn_bias(u - 20)
                    if u == 34:
                        pe.wait_ge(conv_v, 2 * (layer + 1))
                        pe.wait_ge(conv_p, 2 * (layer + 1))
                        channel_mean(cacc, 0).then_inc(mean_made, 1)
                    if u == 36:
                        pe.wait_ge(squared, layer + 1)
                        channel_mean(csq, T).then_inc(var_made, 1)
                    for hd in range(HEADS):
                        if u == SLOT_OF_HEAD[hd]:
                            scores(hd)
                        if u == SLOT_OF_HEAD[hd] + 2:
                            turn_p(hd)
                        if u == SLOT_OF_HEAD[hd] + 3:
                            head_out(hd)

                for u in range(12):
                    a_unit(u)
                v_units(12, 0)
                for u in range(16, 24):
                    a_unit(u)
                    extras(u)
                v_units(24, 2)
                for b in range(3):
                    for pair in range(4):
                        u = BRANCH_UNIT[b] + 3 * pair
                        for m in range(2):
                            a_unit(u + m)
                            extras(u + m)
                        y_unit(u + 2, b, pair)
                        extras(u + 2)
                for k in range(KD):
                    w = unit(base + 64 + k, 1)
                    pe.wait_ge(mrg_lo_s, 4 * layer + k // 2 + 1)
                    by_token(k, w, [mrg_hi, mrg_lo], k == 0, k == KD - 1).then_inc(unit_used, 1)

            def by_token(k, w, parts, first, last):
                for i in range(NT):
                    t = slice(i * P, (i + 1) * P)
                    for n in range(2):
                        c = slice(n * 512, (n + 1) * 512)
                        ins = product(bank[4 + 2 * i + n][:, :], [parts[0][:, k, t], parts[1][:, k, t]],
                                      [w[0][:, 0, c], w[1][:, 0, c]], first, last)
                return ins

            def ffn_up(f, turn=None):
                u = FFN_BASE + (2 + 3 * (f - 1) if f else 0)
                for b in range(2):
                    w = unit(u + b, KD, turn)
                    pe.wait_ge(a_read[b], at(FFN_A_BASE // 2 + f, turn, 4))
                    if f == 0 and b == 0:
                        pe.wait_ge(xt_lo, 16)
                    turned(bank[b][:, 0:T], w, 0, [xT_hi, xT_lo], KD).then_inc(unit_used, 1)

            def ffn_down(f, u, turn=None, first=False, last=False):
                w = unit(u, 1, turn)
                pe.wait_ge(fh_lo_s, at(f + 1, turn, 4))
                by_token(f % 2, w, [fh_hi, fh_lo], first, last).then_inc(unit_used, 1)

            def ffn_step(f, turn=None, first=False):
                ffn_up(f, turn)
                ffn_down(f - 1, FFN_BASE + 2 + 3 * (f - 1) + 2, turn, first)

            def gather(n, e, rounds):
                for r in rounds:
                    pe.wait_ge(pick_ready, at(2 * n + 2, e, 2))
                    if r % 2 == 0 and (n or e is not None or r):
                        pe.wait_ge(slots_a, at(2 * n + r // 2, e, 2))
                    if r % 2 == 1 and (n or e is not None or r > 1):
                        pe.wait_ge(slots_v, at(2 * n + r // 2, e, 2))
                    src, b = (tok_hi, tok_lo)[r // 2], bank[3] if r % 2 == 0 else bank[6]
                    for q in range(4):
                        k = 4 * (r % 2) + q
                        for i in range(NT):
                            ins = pe.matmul(b[:, q * P:(q + 1) * P], src[:, i, k * P:(k + 1) * P],
                                            pick[:, i, :], start=i == 0, stop=i == NT - 1)
                    ins.then_inc(gathered, 1)

            def spread_round(n, q, e=None):
                i, half = divmod(q, 2)
                c = slice(half * 512, (half + 1) * 512)
                if q >= 2:
                    pe.wait_ge(spread_read, at(4 * n + q - 1, e, 4))
                for s, y in enumerate((ye_hi, ye_lo)):
                    ins = pe.matmul(bank[6 + q % 2][:, :], pickT[:, i * P:(i + 1) * P], y[:, c],
                                    start=s == 0, stop=s == 1)
                ins.then_inc(spread, 1)

            def expert(rnd, e):
                u = MOE_BASE + MOE_UNITS * NE * rnd

                def take(view):
                    nonlocal u
                    u += 1
                    return unit(u - 1, view, e, MOE_UNITS)

                def turn_hidden(j):
                    pe.wait_ge(a_read[1], at(MOE_A_USES + NJ * NE * rnd + j + 1, e, NJ))
                    for k in range(4):
                        ins = pe.transpose(bank[2][:, k * P:(k + 1) * P], e_h[:, k * P:(k + 1) * P], ident[:, :])
                    ins.then_inc(eh_made, 1)

                def down(j):
                    for k in range(4):
                        w = take(1)
                        if k == 0:
                            pe.wait_ge(eh_lo_s, at(NJ * NE * rnd + j + 1, e, NJ))
                        for n in range(2):
                            c = slice(n * 512, (n + 1) * 512)
                            ins = product(bank[4 + n][:, :], [eh_hi[:, k, :], eh_lo[:, k, :]],
                                          [w[0][:, 0, c], w[1][:, 0, c]], j == 0 and k == 0, j == NJ - 1 and k == 3)
                        ins.then_inc(unit_used, 1)

                pe.wait_ge(slots_a, at(2 * (9 * rnd) + 2, e, 2))
                pe.wait_ge(slots_v, at(2 * (9 * rnd) + 2, e, 2))
                for j in range(NJ):
                    for b in range(2):
                        pe.wait_ge(a_read[b], at(MOE_A_USES + NJ * NE * rnd + j, e, NJ))
                        for q in range(4):
                            w = take(2)
                            for k in range(2):
                                kk = 2 * q + k
                                ins = product(bank[b][:, :], [p[:, kk, :] for p in slot_parts],
                                              [w[0][:, k, :], w[1][:, k, :]], kk == 0, kk == KD - 1)
                            ins.then_inc(unit_used, 1)
                            if b == 0 and q == 0 and j:
                                turn_hidden(j - 1)
                        if j == 0:
                            if b == 0:
                                pe.wait_ge(ye_lo_s, at(2 * NE * rnd + 1, e, 2))
                                pe.wait_ge(pickT_read, at(NE * rnd + 1, e, 1))
                            spread_round(9 * rnd, 2 * b, e)
                            spread_round(9 * rnd, 2 * b + 1, e)
                    if j == 1:
                        pe.wait_ge(spread_read, at(4 * (9 * rnd) + 4, e, 4))
                        for i in range(NT):
                            ins = pe.transpose(bank[7][:, i * P:(i + 1) * P], pick[:, i, :].bitcast(F32), ident[:, :])
                        ins.then_inc(pickT_made, 1)
                    if j:
                        down(j - 1)
                gather(9 * rnd + 1, e, (0, 1))
                turn_hidden(NJ - 1)
                gather(9 * rnd + 1, e, (2, 3))
                down(NJ - 1)

            pe.wait_ge(consts, 3)
            norm_turn(0)
            mix(0)
            norm_turn(1)
            ffn_up(0)
            ffn_up(1)
            ffn_down(0, FFN_BASE + 4, first=True)
            with pe.Fori(0, 5) as turn:
                for f in range(2, 6):
                    ffn_step(f, turn)
            ffn_down(FT - 1, FFN_BASE + FFN_UNITS - 1, last=True)
            norm_turn(2)
            mix(1)
            norm_turn(3)
            pe.wait_ge(route_read, 4)
            pe.wait_ge(router_in, 16)
            pe.wait_ge(route_const, 2)
            pe.wait_ge(y_read[1], 2 * Y_USES)
            for i in range(NT):
                for k in range(KD):
                    ins = pe.matmul(bank[3][:, 8 * i:8 * i + 8], routeT[:, k, i * P:(i + 1) * P], router[:, k, :],
                                    start=k == 0, stop=k == KD - 1)
            ins.then_inc(logits_made, 1)
            pe.wait_ge(chosen_ready, 2)
            pe.matmul(bank[3][:, 16:24], upper, chosen[:, 0, 0:NE], start=True, stop=True)
            pe.matmul(bank[3][:, 24:32], ones1, chosen[:, 0, 0:NE], start=True, stop=False)
            pe.matmul(bank[3][:, 24:32], upper, chosen[:, 1, 0:NE], start=False, stop=True)
            pe.matmul(bank[3][:, 32:40], ones1, chosen[:, 0, 0:NE], start=True, stop=False)
            pe.matmul(bank[3][:, 32:40], ones1, chosen[:, 1, 0:NE], start=False, stop=True).then_inc(rank_made, 1)
            pe.wait_ge(tok_lo_s, 2)
            pe.wait_ge(flag_ready, 1)

            def experts(rnd):
                if rnd:
                    pe.wait_ge(spread_read, 4 * 9 * rnd)
                gather(9 * rnd, None, range(4))
                with pe.Fori(0, NE) as e:
                    expert(rnd, e)
                pe.wait_ge(ye_lo_s, 2 * NE * (rnd + 1) + 1)
                pe.wait_ge(pickT_read, NE * (rnd + 1) + 1)
                pe.wait_ge(slots_v, 2 * 9 * (rnd + 1))
                for q in range(4):
                    spread_round(9 * rnd + NE, q)

            experts(0)
            again = pe.value_load(flag[0:1, 0:1], min_val=0, max_val=1)
            with pe.If(again > 0):
                experts(1)

        @block.gpsimd
        def _(pool):
            order = Order(pool, pool_step)
            pool.dma_start(par[:, :], params).then_inc(par_loaded, 16)
            order.mark(pool.memset(ident[:, :], 0.0))
            order.mark(pool.memset(anti[:, :], 0.0))
            pool.memset(ones[:, :], 1.0 / CW).then_inc(consts, 1)
            pool.wait_ge(pool_step, 2)
            pool.affine_select(out=anti[:, :], in_=anti[:, :], compare_op=ALU.not_equal, fill=1.0,
                               base=1 - P, pattern=[[1, P]], channel_multiplier=1).then_inc(consts, 1)
            pool.affine_select(out=ident[:, :], in_=ident[:, :], compare_op=ALU.not_equal, fill=1.0,
                               base=0, pattern=[[-1, P]], channel_multiplier=1).then_inc(consts, 1)

            for layer in range(L):
                if layer:
                    pool.wait_ge(rel_out, 16 * layer)
                pool.dma_start(extv[:, 127:127 + N_REL], rel_reversed[layer]).then_inc(rel_in, 16)
                pool.wait_ge(rel_in, 16 * (layer + 1))
                order.mark(pool.tensor_copy(extv[:, 0:127], extv[:, 127:128].to_broadcast([HEADS, 127])))
                order.link(pool.tensor_copy(extv[:, 319:384], extv[:, 318:319].to_broadcast([HEADS, 65])))
                pool.dma_start(scratch[layer], extv[:, 0:384]).then_inc(rel_out, 16)
            pool.wait_ge(rel_out, 16 * L)

            def layer_params(layer):
                pool.dma_start(ln_gb[:, 0, :], sgu_ln_g[layer:layer + 1, :].partition_broadcast(P)).then_inc(sgu_par, 16)
                pool.dma_start(ln_gb[:, 1, :], sgu_ln_b[layer:layer + 1, :].partition_broadcast(P)).then_inc(sgu_par, 16)
                pool.dma_start(bs_b[:, :, :], sgu_bs[layer].partition_broadcast(P)).then_inc(sgu_par, 16)
                pool.dma_start(wsT[:, :, :], sgu_wsT[layer]).then_inc(sgu_par, 16)
                rows = scratch[layer]
                pool.dma_start(bias_t[:, :, :], bass.AP(rows.tensor, rows.offset,
                                                        [[1, P], [384, HEADS], [1, 2 * P]])).then_inc(bias_in, 16)
                pool.wait_ge(sgu_par, 64 * (layer + 1))
                pool.memset(wsT[64:128, :, 0:64], 0.0).then_inc(sgu_mask, 1)
                pool.wait_ge(sgu_mask, layer + 1)
                pool.wait_ge(bias_in, 16 * (layer + 1))
                pool.memset(bias_t[64:128, :, 192:256], NEG).then_inc(bias_ready, 1)
                pool.wait_ge(bias_ready, layer + 1)

            def conv_taps(layer):
                pool.wait_ge(par_loaded, 16)
                pool.wait_ge(a_read[1], A_BASE[layer] // 2 + 4)
                w = C_CONVW + TAPS * 2
                order.link(pool.tensor_scalar(cacc[:, 2, :], cin[:, 2, 0:T], pcol(layer, w), None, ALU.mult))
                for k in range(1, TAPS):
                    order.link(pool.tensor_scalar(tap_pool, cin[:, 2, k:k + T], pcol(layer, w + k), None, ALU.mult))
                    order.link(pool.tensor_tensor(cacc[:, 2, :], cacc[:, 2, :], tap_pool, ALU.add))
                    pool.wait_ge(tap_made, TAPS * layer + k + 1)
                    pool.tensor_tensor(cacc[:, 3, :], cacc[:, 3, :], tap_act[:, k % 2, :], ALU.add)\
                        .then_inc(tap_added, 1)
                    pool.wait_ge(tap_added, (TAPS - 1) * layer + k)
                for c in (2, 3):
                    pool.tensor_scalar(cacc[:, c, :], cacc[:, c, :], 0.5, pcol(layer, C_CONVB + c),
                                       ALU.mult, ALU.add).then_inc(conv_p, 1)

            layer_params(0)
            conv_taps(0)
            pool.wait_ge(um_lo, 1)
            pool.wait_ge(o_lo, 4)
            layer_params(1)
            conv_taps(1)
            pool.wait_ge(o_lo, 4 * L)
            pool.dma_start(g_ffn_b, ffn_norm_g[1:2, :].partition_broadcast(P)).then_inc(wide_loaded, 16)
            pool.dma_start(g_fin_b, final_norm_g.unsqueeze(0).partition_broadcast(P)).then_inc(wide_loaded, 16)
            pool.dma_start(router, moe_router[0].rearrange("(k p) e -> p k e", p=P)).then_inc(router_in, 16)
            order.mark(pool.iota(iota_i[:, :], [[1, P]], base=0, channel_multiplier=0))
            order.link(pool.memset(ones1, 1.0))
            pool.affine_select(out=upper, in_=ones1, compare_op=ALU.is_gt, fill=0.0,
                               base=0, pattern=[[1, P]], channel_multiplier=-1).then_inc(route_const, 1)
            pool.tensor_copy(iota, iota_i[:, :]).then_inc(route_const, 1)


_OUTS = [((1, 256, 1024), "float32")]


def kernel(**inputs):
    import numpy as _np
    import concourse.bacc as _bacc
    from concourse import mybir as _mybir
    from concourse.bass_utils import run_bass_kernel_spmd as _run

    a = {k: _np.asarray(v) for k, v in inputs.items()}

    def columns(v):
        return v.reshape(-1, P).T

    par = []
    for layer in range(L):
        taps = a["conv_dw_w"][layer].reshape(TAPS, CG, P).transpose(2, 1, 0).reshape(P, CG * TAPS)
        par += [columns(a["mix_norm_g"][layer]), columns(a["b_gate"][layer]), taps,
                columns(a["conv_dw_b"][layer]), columns(a["conv_ln_g"][layer]),
                columns(a["conv_ln_b"][layer]), columns(a["ffn_norm_g"][layer])]
    feed = {k: a[k] for k in ("x", "w_in", "conv_out_w", "sgu_out_w", "attn_out_w", "w_out", "ffn_w_gate",
                              "ffn_w_up", "ffn_w_down", "moe_router", "moe_w_gate", "moe_w_up", "moe_w_down")}
    feed["params"] = _np.concatenate(par, axis=1)
    feed["sgu_ln_g"], feed["sgu_ln_b"] = a["sgu_ln_g"], a["sgu_ln_b"]
    feed["sgu_wsT"] = a["sgu_ws"].transpose(0, 3, 1, 2)
    feed["sgu_bs"] = a["sgu_bs"]
    feed["rel_reversed"] = a["attn_rel_bias"][:, :, ::-1]
    feed["ffn_norm_g"], feed["final_norm_g"] = a["ffn_norm_g"], a["final_norm_g"]

    nc = _bacc.Bacc("TRN2", target_bir_lowering=False, num_devices=1)
    arrays, args = {}, []
    for name, v in feed.items():
        v = _np.ascontiguousarray(v)
        arrays[f"in_{name}_dram"] = v
        args.append(nc.dram_tensor(f"in_{name}_dram", v.shape, _mybir.dt.from_np(v.dtype), kind="ExternalInput").ap())
    for i, (shape, dtype) in enumerate(_OUTS):
        dt = _mybir.dt.from_np(_np.dtype(dtype))
        args.append(nc.dram_tensor(f"out_{i}_dram", shape, dt, kind="ExternalOutput").ap())
    trunk(nc, *args)
    r = _run(nc, [arrays], core_ids=[0])
    got = tuple(r.results[0][f"out_{i}_dram"] for i in range(len(_OUTS)))
    return got[0]
```

```python
from contextlib import ExitStack

import concourse.bass as bass
from concourse import mybir

F32 = mybir.dt.float32
F32R = mybir.dt.float32r
I32 = mybir.dt.int32
U32 = mybir.dt.uint32
ACT = mybir.ActivationFunctionType
ALU = mybir.AluOpType
AX = mybir.AxisListType

P = 128
D, T, L = 1024, 256, 2
KD, NT = D // P, T // P
CW, TAPS, CG = 512, 31, 4
HEADS, HD = 8, 64
CHUNK, N_REL = 64, 192
FT = 2816 // P
NE, FE = 8, 3584
NJ = FE // 512
EPS = 1e-6
NEG = -1e30
RSQRT_SEED = float(0x5F3759DF)

UNIT = 1024
RAW, SPLIT, AHEAD = 12, 6, 5
MIX_UNITS, FFN_UNITS, MOE_UNITS = 72, 3 * FT, 12 * NJ
MIX_A, FFN_A = 44, 2 * FT
MIX_BASE = [0, MIX_UNITS + FFN_UNITS]
FFN_BASE = MIX_UNITS
MOE_BASE = MIX_BASE[1] + MIX_UNITS
A_BASE = [0, MIX_A + FFN_A]
FFN_A_BASE = MIX_A
MOE_A_USES = (A_BASE[1] + MIX_A) // 2
Y_USES = 9
BRANCH_UNIT = [28, 40, 52]
BRANCH_GATE = [8, 16, 0]
SLOT_OF_HEAD = [21 + 2 * h for h in range(HEADS)]
OUT_OF_HEAD = [max(28, 21 + 2 * h + 6 - h % 2) for h in range(HEADS)]

C_MIXG, C_GATEB, C_CONVW, C_CONVB, C_LNG, C_LNB, C_FFNG = 0, 8, 32, 156, 160, 164, 168
C_LAYER = 176


def at(constant, turn, stride):
    return constant if turn is None else turn * stride + constant


class Order:

    def __init__(self, eng, sem):
        self.eng, self.sem, self.n, self.turn, self.stride = eng, sem, 0, None, 0

    def value(self, back=0):
        return at(self.n - back, self.turn, self.stride)

    def mark(self, ins):
        ins.then_inc(self.sem, 1)
        self.n += 1

    def link(self, ins):
        self.mark(ins)
        self.eng.wait_ge(self.sem, self.value())

    def enter(self, turn, stride):
        self.turn, self.stride, self.at_entry = turn, stride, self.n

    def leave(self, turns):
        assert self.n - self.at_entry == self.stride, (self.n - self.at_entry, self.stride)
        self.n = self.at_entry + self.stride * turns
        self.turn, self.stride = None, 0


def trunk(nc, x, w_in, conv_out_w, sgu_out_w, attn_out_w, w_out, ffn_w_gate, ffn_w_up, ffn_w_down,
          moe_router, moe_w_gate, moe_w_up, moe_w_down, params, sgu_ln_g, sgu_ln_b, sgu_wsT, sgu_bs,
          rel_reversed, ffn_norm_g, final_norm_g, out):
    with ExitStack() as ctx:
        def sb(name, shape, dt=F32):
            return ctx.enter_context(nc.sbuf_tensor(name, shape, dt))

        def sem(name):
            return ctx.enter_context(nc.semaphore(name))

        raw = sb("raw", [P, RAW, UNIT])
        whi = sb("whi", [P, SPLIT, UNIT], F32R)
        wlo = sb("wlo", [P, SPLIT, UNIT], F32R)

        x_hi = sb("x_hi", [P, 2048], F32R)
        x_lo = sb("x_lo", [P, 2048], F32R)
        br_ab = sb("br_ab", [P, 4096], F32R)
        br_c = sb("br_c", [P, 2048], F32R)
        xT_hi = x_hi[:, :].rearrange("p (k t) -> p k t", k=KD)
        xT_lo = x_lo[:, :].rearrange("p (k t) -> p k t", k=KD)

        def quarter(a, n, k):
            return a[:, n * 1024:(n + 1) * 1024].rearrange("p (k t) -> p k t", k=k)

        sgu_hi, sgu_lo = quarter(br_ab, 0, 4), quarter(br_ab, 1, 4)
        attn_hi, attn_lo = quarter(br_ab, 2, 4), quarter(br_ab, 3, 4)
        conv_hi, conv_lo = quarter(br_c, 0, 4), quarter(br_c, 1, 4)
        branch_parts = [(sgu_hi, sgu_lo), (attn_hi, attn_lo), (conv_hi, conv_lo)]
        mrg_hi = br_ab[:, 0:2048].rearrange("p (k t) -> p k t", k=KD)
        mrg_lo = br_ab[:, 2048:4096].rearrange("p (k t) -> p k t", k=KD)
        fh_hi = br_c[:, 0:512].rearrange("p (b t) -> p b t", b=2)
        fh_lo = br_c[:, 512:1024].rearrange("p (b t) -> p b t", b=2)
        tok_hi = x_hi[:, :].rearrange("p (i d) -> p i d", i=NT)
        tok_lo = x_lo[:, :].rearrange("p (i d) -> p i d", i=NT)
        slot_parts = [quarter(br_ab, 0, KD), quarter(br_ab, 1, KD)]
        ye_hi, ye_lo = br_ab[:, 2048:3072], br_ab[:, 3072:4096]
        eh_hi = br_c[:, 0:512].rearrange("p (k t) -> p k t", k=4)
        eh_lo = br_c[:, 512:1024].rearrange("p (k t) -> p k t", k=4)
        eh2_hi = br_ab[:, 0:512].rearrange("p (k t) -> p k t", k=4)
        eh2_lo = br_ab[:, 512:1024].rearrange("p (k t) -> p k t", k=4)
        pick = br_c[:, 1024:1280].rearrange("p (i s) -> p i s", i=NT)
        pickT = br_c[:, 1280:1536]

        h = sb("h", [P, NT, D])
        xn = sb("xn", [P, 2048])
        xn_tok = xn[:, :].rearrange("p (i d) -> p i d", i=NT)
        merged = xn[:, :].rearrange("p (k t) -> p k t", k=KD)
        cin = sb("cin", [P, CG, TAPS - 1 + T])
        cacc = sb("cacc", [P, CG, T])
        uT = sb("uT", [P, 4, T])
        gate_t = uT[:, :, :].rearrange("p (b m) t -> p b m t", b=2)
        v_sgu = sb("v_sgu", [P, 1024])
        v_tok = v_sgu[:, :].rearrange("p (i c) -> p i c", i=NT)
        um = v_sgu[:, :].rearrange("p (g t) -> p g t", g=4)
        csq = um
        qT = sb("qT", [P, 4, T])
        kT = sb("kT", [P, 4, T])
        v_att = sb("v_att", [P, NT, HEADS * HD])
        bias_t = sb("bias_t", [P, HEADS, 2 * P])
        routeT = bias_t[:, :, :]
        squares = bias_t[:, :, :].rearrange("p (i a) t -> p i (a t)", i=NT)
        probs = sb("probs", [P, 4 * 384])
        S = probs[:, 0:768].rearrange("p (b n) -> p b n", b=2)
        pT = probs[:, 768:1536].rearrange("p (b n) -> p b n", b=2)
        ln_gb = probs[:, 0:1024].rearrange("p (b n) -> p b n", b=2)
        stat = sb("stat", [P, 4, T])
        sig, mtmp = stat[:, 0:2, :], qT[:, 0:2, :]
        tile_sum = stat[:, 3, :]
        tap_prod = stat[:, :, :].rearrange("p (b c) t -> p b c t", b=2)
        bs_b = sb("bs_b", [P, 4, P])
        wsT = sb("wsT", [P, 4, P])
        e_sl, e_h = uT[:, 0:2, :].rearrange("p a t -> p (a t)"), uT[:, 2:4, :].rearrange("p a t -> p (a t)")
        f_sl, f_h = uT[:, 0:2, :], uT[:, 2:4, :]
        g_ffn_b = qT[:, :, :].rearrange("p a t -> p (a t)")
        g_fin_b = kT[:, :, :].rearrange("p a t -> p (a t)")

        ident = sb("ident", [P, P])
        ones = sb("ones", [P, P])
        par = sb("par", [P, L * C_LAYER])
        par_half = sb("par_half", [P, L * C_LAYER])
        small = sb("small", [P, 64])
        root = sb("root", [P, NT, 4])
        rms = sb("rms", [P, NT])
        router = v_att[:, 0, 0:64].rearrange("p (k e) -> p k e", k=KD)
        upper = v_att[:, 0, 128:256]
        ones1 = v_att[:, 0, 256:384]
        iota = v_att[:, 1, 0:128]
        logitsT = v_att[0:NE, 1, 256:512]
        top = sb("top", [P, NT, 8])
        topi = sb("topi", [P, NT, 8], U32)
        flag = sb("flag", [P, 1], I32)
        extv = bias_t[0:L * HEADS, 0:2, :].rearrange("p a b -> p (a b)")
        iota_i = v_att[:, 1, 128:256].bitcast(I32)
        chosen = sb("chosen", [P, NT, NE + 1])
        rank = sb("rank", [P, NT, NE + 1])
        slot = sb("slot", [P, NT, NE + 1])
        weight = sb("weight", [P, NT, NE + 1])
        sel = sb("sel", [P, NT, 2, NE])
        best = small[:, 46:50].rearrange("p (i r) -> p i r", i=NT)
        share = small[:, 50:54].rearrange("p (i r) -> p i r", i=NT)
        scratch = nc.dram_tensor("rel_rows", (L * HEADS, P, 384), F32).ap()

        bank = [ctx.enter_context(nc.psum_tensor(f"bank{n}", [P, 512], F32)) for n in range(8)]

        raw_loaded = [sem(f"raw_loaded{n}") for n in range(RAW)]
        hi_made, lo_made, unit_used = sem("hi_made"), sem("lo_made"), sem("unit_used")
        a_read = [sem("bank0_read"), sem("bank1_read")]
        y_read = [sem("bank2_read"), sem("bank3_read")]
        x_loaded, par_loaded = [sem("x_loaded0"), sem("x_loaded1")], sem("par_loaded")
        consts, par_ready = sem("consts"), sem("par_ready")
        sgu_par, sgu_mask = sem("sgu_par"), sem("sgu_mask")
        rel_in, rel_out, bias_in, bias_ready = (
            sem("rel_in"), sem("rel_out"), sem("bias_in"), sem("bias_ready"))
        sumsq, xn_ready, xt_made, xt_hi, xt_lo = (
            sem("sumsq"), sem("xn_ready"), sem("xt_made"), sem("xt_hi"), sem("xt_lo"))
        first_tile_made, h_ready = sem("first_tile_made"), sem("h_ready")
        conv_v, conv_p = sem("conv_v"), sem("conv_p")
        tap_made, tap_added, tiles_summed = sem("tap_made"), sem("tap_added"), sem("tiles_summed")
        mean_made, centred, squared, var_made, conv_norm, conv_act, conv_y, conv_hi_s, conv_lo_s = (
            sem("mean_made"), sem("centred"), sem("squared"), sem("var_made"), sem("conv_norm"),
            sem("conv_act"), sem("conv_y"), sem("conv_hi"), sem("conv_lo"))
        vn_ready, mix_made, um_ready, um_hi, um_lo = (
            sem("vn_ready"), sem("mix_made"), sem("um_ready"), sem("um_hi"), sem("um_lo"))
        s_made, s_read, s_max, s_exp, p_ready, pt_made, pt_read, o_made, o_hi, o_lo = (
            sem("s_made"), sem("s_read"), sem("s_max"), sem("s_exp"), sem("p_ready"),
            sem("pt_made"), sem("pt_read"), sem("o_made"), sem("o_hi"), sem("o_lo"))
        mrg_ready, mrg_hi_s, mrg_lo_s = sem("mrg_ready"), sem("mrg_hi"), sem("mrg_lo")
        fh_hi_s, fh_lo_s = sem("fh_hi"), sem("fh_lo")
        wide_loaded, xg_ready, tok_hi_s, tok_lo_s, route_read = (
            sem("wide_loaded"), sem("xg_ready"), sem("tok_hi"), sem("tok_lo"), sem("route_read"))
        logitsT_made, logitsT_read = sem("logitsT_made"), sem("logitsT_read")
        rank_read, total_made = sem("rank_read"), sem("total_made")
        router_in, route_const, logits_made, gap_ready, gap_exp, chosen_ready, rank_made, flag_ready = (
            sem("router_in"), sem("route_const"), sem("logits_made"), sem("gap_ready"), sem("gap_exp"),
            sem("chosen_ready"), sem("rank_made"), sem("flag_ready"))
        pick_ready, gathered, slots_a, slots_v = (
            sem("pick_ready"), sem("gathered"), sem("slots_a"), sem("slots_v"))
        pickT_made, pickT_read = sem("pickT_made"), sem("pickT_read")
        y_half_made = sem("y_half_made")
        eh_made, eh_hi_s, eh_lo_s = sem("eh_made"), sem("eh_hi"), sem("eh_lo")
        ye_hi_s, ye_lo_s, spread, spread_read = (
            sem("ye_hi"), sem("ye_lo"), sem("spread"), sem("spread_read"))
        last_spread, last_spread_read = sem("last_spread"), sem("last_spread_read")
        final_step, gained, rms_ready = sem("final_step"), sem("gained"), sem("rms_ready")
        out_ready, out_stored = [sem("out_ready0"), sem("out_ready1")], sem("out_stored")
        act_step, dve_step, pool_step = sem("act_step"), sem("dve_step"), sem("pool_step")

        block = ctx.enter_context(nc.Block())

        def pcol(layer, c, n=1, half=False):
            a = layer * C_LAYER + c
            return (par_half if half else par)[:, a:a + n]

        @block.sync
        def _(sp):
            def load(u, view, src, turn=None):
                if u >= RAW:
                    sp.wait_ge(lo_made, at(u - RAW + 1, turn, 12))
                dst = raw[:, u % RAW, :]
                if view > 1:
                    dst = dst.rearrange("p (k n) -> p k n", k=view)
                sp.dma_start(dst, src).then_inc(raw_loaded[u % RAW], 16)

            for i in range(NT):
                sp.dma_start(h[:, i, :], x[0, i * P:(i + 1) * P, :]).then_inc(x_loaded[i], 16)

            def load_mix(layer):
                base = MIX_BASE[layer]
                w = w_in[layer].rearrange("(k p) n -> p k n", p=P)
                u = base

                def columns(c):
                    nonlocal u
                    load(u, KD, w[:, :, c:c + P])
                    u += 1

                def rows(c):
                    nonlocal u
                    for k in range(0, KD, 2):
                        load(u, 2, w[:, k:k + 2, c:c + 512])
                        u += 1

                for c in range(CG):
                    columns(CW + c * P)
                    columns(c * P)
                for c in range(4):
                    columns(1024 + c * P)
                rows(1536)
                for c in range(4):
                    columns(2048 + c * P)
                    columns(2560 + c * P)
                rows(3072)
                outs = [sgu_out_w, attn_out_w, conv_out_w]
                for b in range(3):
                    wo = outs[b][layer].rearrange("(k p) n -> p k n", p=P)
                    for pair in range(4):
                        for m in range(2):
                            columns(3584 + (BRANCH_GATE[b] + 2 * pair + m) * P)
                        load(u, 4, wo[:, :, pair * 256:pair * 256 + 256])
                        u += 1
                for k in range(KD):
                    load(u, 1, w_out[layer, k * P:(k + 1) * P, :])
                    u += 1
                assert u == base + MIX_UNITS

            wg = ffn_w_gate[0].rearrange("(k p) n -> p k n", p=P)
            wu = ffn_w_up[0].rearrange("(k p) n -> p k n", p=P)
            wd = ffn_w_down[0].rearrange("(f p) n -> f p n", p=P)

            def load_ffn(f, turn=None, down=True):
                u = FFN_BASE + (2 + 3 * (f - 1) if f else 0)
                c = at(f * P, turn, 4 * P)
                load(u, KD, wg[:, :, bass.ds(c, P)], turn)
                load(u + 1, KD, wu[:, :, bass.ds(c, P)], turn)
                if down:
                    src = wd[bass.ds(at(f - 1, turn, 4), 1)].rearrange("a p n -> (a p) n")
                    load(u + 2, 1, src, turn)

            def load_expert(rnd, e):
                u = MOE_BASE + MOE_UNITS * NE * rnd
                g = moe_w_gate[0].rearrange("e (k p) n -> e p k n", p=P)[bass.ds(e, 1)].rearrange("a p k n -> (a p) k n")
                up = moe_w_up[0].rearrange("e (k p) n -> e p k n", p=P)[bass.ds(e, 1)].rearrange("a p k n -> (a p) k n")
                dn = moe_w_down[0].rearrange("e (f p) n -> e p f n", p=P)[bass.ds(e, 1)].rearrange("a p f n -> (a p) f n")

                def one(view, src):
                    nonlocal u
                    sp.wait_ge(lo_made, at(u - RAW + 1, e, MOE_UNITS))
                    dst = raw[:, u % RAW, :]
                    sp.dma_start(dst.rearrange("p (k n) -> p k n", k=view), src).then_inc(raw_loaded[u % RAW], 16)
                    u += 1

                def down(j):
                    for k in range(4):
                        one(1, dn[:, 4 * j + k:4 * j + k + 1, :])

                for j in range(NJ):
                    for w in (g, up):
                        for k in range(0, KD, 2):
                            one(2, w[:, k:k + 2, j * 512:(j + 1) * 512])
                    if j:
                        down(j - 1)
                down(NJ - 1)

            load_mix(0)
            load_ffn(0, down=False)
            with sp.Fori(0, 5) as turn:
                for f in range(1, 5):
                    load_ffn(f, turn)
            load_ffn(FT - 1)
            load(FFN_BASE + FFN_UNITS - 1, 1, wd[FT - 1])
            load_mix(1)
            with sp.Fori(0, NE) as e:
                load_expert(0, e)
            sp.wait_ge(flag_ready, 1)
            again = sp.value_load(flag[0:1, 0:1], min_val=0, max_val=1)
            with sp.If(again > 0):
                with sp.Fori(0, NE) as e:
                    load_expert(1, e)
            o = out.rearrange("b (i p) d -> (b i) p d", p=P)
            for q in range(2 * NT):
                half, i = divmod(q, 2)
                c = slice(half * 512, (half + 1) * 512)
                sp.wait_ge(out_ready[i], half + 1)
                sp.dma_start(o[i, :, c], xn_tok[:, i, c]).then_inc(out_stored, 16)
            sp.wait_ge(out_stored, 16 * 2 * NT)

        @block.scalar
        def _(act):
            order = Order(act, act_step)

            def split_hi(u, turn=None, stride=12):
                act.wait_ge(raw_loaded[u % RAW], at(16 * (u // RAW + 1), turn, 16 * stride // RAW))
                if u >= SPLIT or turn is not None:
                    act.wait_ge(unit_used, at(u - SPLIT + 1, turn, stride))
                act.activation(whi[:, u % SPLIT, :], raw[:, u % RAW, :], ACT.Copy).then_inc(hi_made, 1)

            def norm_sums(n, tiles=(0, 1)):
                for i in tiles:
                    if n == 0:
                        act.wait_ge(x_loaded[i], 16)
                    else:
                        act.wait_ge(h_ready, 2 * (n - 1) + i + 1)
                    act.activation(xn_tok[:, i, :], h[:, i, :], ACT.Square,
                                   accum_out=small[:, i:i + 1]).then_inc(sumsq, 1)

            def norm_hi(n, gain):
                for k in range(KD):
                    act.wait_ge(xt_made, 4 * n + k // 2 + 1)
                    act.activation(xT_hi[:, k, :], bank[4 + k // 2][:, (k % 2) * T:(k % 2 + 1) * T],
                                   ACT.Copy, scale=gain[:, k:k + 1]).then_inc(xt_hi, 1)

            def mix(layer):
                base, heads, y0 = MIX_BASE[layer], HEADS * layer, Y_USES * layer
                uses0 = A_BASE[layer] // 2

                def used(u):
                    act.wait_ge(unit_used, base + u + 1)

                def tap(k):
                    if k == 0:
                        act.wait_ge(a_read[1], uses0 + 4)
                    if k >= 3:
                        act.wait_ge(tap_added, (TAPS - 1) * layer + k - 2)
                    for c in (2, 3):
                        dst = tap_prod[:, k % 2, c - 2, :] if k else cacc[:, c, :]
                        act.activation(dst, cin[:, c, k:k + T], ACT.Copy,
                                       scale=pcol(layer, C_CONVW + TAPS * c + k)).then_inc(tap_made, 1)

                taps_done = 0
                for u in range(MIX_UNITS - 3):
                    split_hi(base + u + AHEAD)
                    while u >= 8 and taps_done < min(TAPS, u - 7):
                        tap(taps_done)
                        taps_done += 1
                    if u < 8 and u % 2 == 0:
                        c = u // 2
                        if c >= 2:
                            act.wait_ge(a_read[1], uses0 + c - 1)
                        used(u)
                        act.activation(sig[:, c % 2, :], bank[0][:, 0:T], ACT.Tanh, scale=0.5)\
                           .then_inc(a_read[0], 1)
                    elif 8 <= u < 12:
                        used(u)
                        act.activation(uT[:, u - 8, :], bank[u % 2][:, 0:T], ACT.Gelu).then_inc(a_read[u % 2], 1)
                    elif u == 15:
                        used(u)
                        for i in range(NT):
                            act.activation(v_tok[:, i, :], bank[2 + i][:, :], ACT.Gelu).then_inc(y_read[i], 1)
                    elif 16 <= u < 24:
                        used(u)
                        dst = (kT if u % 2 else qT)[:, (u - 16) // 2, :]
                        act.activation(dst, bank[u % 2][:, 0:T], ACT.Copy).then_inc(a_read[u % 2], 1)
                    elif u == 27:
                        used(u)
                        for i in range(NT):
                            act.activation(v_att[:, i, :], bank[2 + i][:, :], ACT.Copy).then_inc(y_read[i], 1)
                    if u == 20:
                        act.wait_ge(um_ready, layer + 1)
                        act.activation(sgu_hi, um, ACT.Copy).then_inc(um_hi, 1)
                    for b in range(3):
                        g = u - BRANCH_UNIT[b]
                        if 0 <= g < 12 and g % 3 < 2:
                            m, yi = 2 * (g // 3) + g % 3, 4 * b + g // 3
                            parity = m % 2
                            if yi >= 2:
                                act.wait_ge(y_read[yi % 2], y0 + 3 + yi // 2)
                            used(u)
                            if layer == b == g == 0:
                                act.wait_ge(par_ready, 1)
                            act.activation(gate_t[:, yi % 2, m % 2, :], bank[parity][:, 0:T], ACT.Tanh,
                                           scale=0.5, bias=pcol(layer, C_GATEB + BRANCH_GATE[b] + m, half=True))\
                               .then_inc(a_read[parity], 1)
                    for hd in range(HEADS):
                        s = SLOT_OF_HEAD[hd]
                        if u == s + 1:
                            act.wait_ge(s_max, heads + hd + 1)
                            for q, (a, b) in enumerate(((0, 256), (256, 384))):
                                act.activation(S[:, hd % 2, a:b], S[:, hd % 2, a:b], ACT.Exp,
                                               bias=small[:, 8 + 2 * (hd % 2) + q:9 + 2 * (hd % 2) + q],
                                               accum_out=small[:, 12 + 2 * (hd % 2) + q:13 + 2 * (hd % 2) + q])\
                                   .then_inc(s_exp, 1)
                        if u == s + 3:
                            act.wait_ge(pt_made, heads + hd + 1)
                            if hd >= 2:
                                act.wait_ge(o_made, heads + hd - 1)
                            act.activation(pT[:, hd % 2, :], bank[6][:, 0:384], ACT.Copy).then_inc(pt_read, 1)
                        if u == OUT_OF_HEAD[hd] and hd % 2:
                            act.wait_ge(o_made, heads + hd + 1)
                            act.activation(attn_hi[:, hd // 2, :], bank[7][:, 0:T], ACT.Copy).then_inc(o_hi, 1)
                    if u == 42:
                        act.wait_ge(centred, layer + 1)
                        act.activation(csq, cacc[:, :, :], ACT.Square).then_inc(squared, 1)
                    if u == 46:
                        act.wait_ge(conv_norm, layer + 1)
                        for c in range(CG):
                            order.mark(act.activation(csq[:, c, :], cacc[:, c, :], ACT.Tanh,
                                                      scale=pcol(layer, C_LNG + c, half=True),
                                                      bias=pcol(layer, C_LNB + c, half=True)))
                    if u == 47:
                        act.wait_ge(act_step, order.value())
                        for c in range(CG):
                            act.activation(cacc[:, c, :], cacc[:, c, :], ACT.Identity,
                                           scale=pcol(layer, C_LNG + c), bias=pcol(layer, C_LNB + c))\
                               .then_inc(conv_act, 1)
                    if u == 49:
                        act.wait_ge(conv_y, layer + 1)
                        act.activation(conv_hi, cacc[:, :, :], ACT.Copy, scale=0.5).then_inc(conv_hi_s, 1)
                    if u >= BRANCH_UNIT[2] and (u - BRANCH_UNIT[2]) % 3 == 2 and u < 64:
                        pair = (u - BRANCH_UNIT[2]) // 3
                        act.wait_ge(mrg_ready, 4 * layer + pair + 1)
                        act.activation(mrg_hi[:, 2 * pair:2 * pair + 2, :], merged[:, 2 * pair:2 * pair + 2, :],
                                       ACT.Copy, scale=0.5).then_inc(mrg_hi_s, 1)

            def ffn_silu(f, turn=None):
                u = FFN_BASE + (2 + 3 * (f - 1) if f else 0)
                act.wait_ge(unit_used, at(u + 1, turn, 12))
                if f >= 2 or turn is not None:
                    act.wait_ge(a_read[1], at(FFN_A_BASE // 2 + f - 1, turn, 4))
                act.activation(f_sl[:, f % 2, :], bank[0][:, 0:T], ACT.Silu).then_inc(a_read[0], 1)

            def ffn_hi(f, turn=None):
                act.wait_ge(a_read[1], at(FFN_A_BASE // 2 + f + 1, turn, 4))
                if f >= 2 or turn is not None:
                    act.wait_ge(unit_used, at(FFN_BASE + 2 + 3 * (f - 2) + 3, turn, 12))
                act.activation(fh_hi[:, f % 2, :], f_h[:, f % 2, :], ACT.Copy).then_inc(fh_hi_s, 1)

            def ffn_step(f, turn=None):
                u = FFN_BASE + 2 + 3 * (f - 1)
                split_hi(u + AHEAD, turn)
                split_hi(u + 1 + AHEAD, turn)
                ffn_silu(f, turn)
                split_hi(u + 2 + AHEAD, turn)
                ffn_hi(f, turn)

            def expert(rnd, e, last=False):
                u0 = MOE_BASE + MOE_UNITS * NE * rnd
                for k in range(MOE_UNITS):
                    if not last or k + AHEAD < MOE_UNITS:
                        split_hi(u0 + k + AHEAD, e, MOE_UNITS)
                    j, q = (0, k) if k < 8 else ((k - 8) // 12 + 1, (k - 8) % 12)
                    if j < NJ and q == 1 and j:
                        expert_hi(rnd, e, j - 1)
                    if j < NJ and q == 3:
                        c = NJ * (NE * rnd) + j
                        act.wait_ge(unit_used, at(u0 + k + 1, e, MOE_UNITS))
                        act.wait_ge(a_read[1], at(MOE_A_USES + c, e, NJ))
                        act.activation(e_sl, bank[0][:, :], ACT.Silu).then_inc(a_read[0], 1)
                    if j == 1 and q == 8:
                        act.wait_ge(pickT_made, at(NE * rnd + 1, e, 1))
                        act.activation(pickT, bank[7][:, 0:T], ACT.Copy).then_inc(pickT_read, 1)
                    if j == NJ - 1 and q == 7:
                        if not last:
                            gather_read(NE * rnd + 1, e, (0,))
                            expert_hi(rnd, e, NJ - 1)
                            gather_read(NE * rnd + 1, e, (2,))
                    if j == NJ - 1 and q == 9 and last:
                        expert_hi(rnd, e, NJ - 1, eh2_hi)
                for n in range(2):
                    if n == 0:
                        act.wait_ge(y_half_made, at(NE * rnd + 1, e, 1))
                    else:
                        act.wait_ge(unit_used, at(u0 + MOE_UNITS, e, MOE_UNITS))
                    act.activation(ye_hi[:, n * 512:(n + 1) * 512], bank[4 + n][:, :], ACT.Copy).then_inc(ye_hi_s, 1)

            def expert_hi(rnd, e, j, dst=eh_hi):
                act.wait_ge(eh_made, at(NJ * NE * rnd + j + 1, e, NJ))
                act.activation(dst, bank[2][:, :], ACT.Copy).then_inc(eh_hi_s, 1)

            def gather_read(n, e=None, rounds=(0, 2)):
                for r in rounds:
                    act.wait_ge(gathered, at(4 * n + r + 1, e, 4))
                    act.activation(slot_parts[r // 2][:, 0:4, :], bank[3][:, :], ACT.Copy).then_inc(slots_a, 1)

            norm_sums(0)
            for u in range(2):
                split_hi(u)
            act.wait_ge(par_loaded, 16)
            norm_hi(0, pcol(0, C_MIXG, 8))
            for u in range(2, AHEAD):
                split_hi(u)

            def after_mix(layer):
                norm_sums(2 * layer + 1, (0,))
                for u in range(3):
                    split_hi(MIX_BASE[layer] + MIX_UNITS + 2 + u)
                norm_sums(2 * layer + 1, (1,))

            mix(0)
            after_mix(0)
            norm_hi(1, pcol(0, C_FFNG, 8))
            split_hi(FFN_BASE + AHEAD)
            split_hi(FFN_BASE + 1 + AHEAD)
            ffn_silu(0)
            ffn_hi(0)
            with act.Fori(0, 5) as turn:
                for f in range(1, 5):
                    ffn_step(f, turn)
            ffn_step(FT - 1)
            split_hi(FFN_BASE + FFN_UNITS - 1 + AHEAD)
            norm_sums(2)
            norm_hi(2, pcol(1, C_MIXG, 8))
            mix(1)
            after_mix(1)
            for i in range(NT):
                act.wait_ge(xg_ready, i + 1)
                act.activation(tok_hi[:, i, :], xn_tok[:, i, :], ACT.Copy).then_inc(tok_hi_s, 1)
            for k in range(4):
                act.wait_ge(xt_made, 4 * 3 + k + 1)
                act.activation(routeT[:, 2 * k:2 * k + 2, :], bank[4 + k][:, :].rearrange("p (a t) -> p a t", a=2),
                               ACT.Copy).then_inc(route_read, 1)
            act.wait_ge(gap_ready, 1)
            act.activation(small[:, 24:26], small[:, 20:22], ACT.Exp).then_inc(gap_exp, 1)

            def experts(rnd):
                gather_read(NE * rnd)
                with act.Fori(0, NE - 1) as e:
                    expert(rnd, e)
                expert(rnd, NE - 1, last=True)

            experts(0)
            act.wait_ge(flag_ready, 1)
            again = act.value_load(flag[0:1, 0:1], min_val=0, max_val=1)
            with act.If(again > 0):
                for u in range(AHEAD):
                    split_hi(MOE_BASE + MOE_UNITS * NE + u)
                experts(1)
            for i in range(NT):
                act.wait_ge(last_spread_read, 2 * i + 2)
                act.activation(squares[:, i, :], h[:, i, :], ACT.Square,
                               accum_out=small[:, i:i + 1]).then_inc(sumsq, 1)
            act.wait_ge(gained, 1)
            act.wait_ge(rms_ready, 1)
            for half in range(2):
                c = slice(half * 512, (half + 1) * 512)
                act.activation(xn_tok[:, 0, c], xn_tok[:, 0, c], ACT.Copy, scale=rms[:, 0:1]).then_inc(out_ready[0], 1)

        @block.vector
        def _(dve):
            order = Order(dve, dve_step)

            def split_lo(u, turn=None, stride=12):
                dve.wait_ge(hi_made, at(u + 1, turn, stride))
                dve.tensor_tensor(wlo[:, u % SPLIT, :], raw[:, u % RAW, :], whi[:, u % SPLIT, :],
                                  ALU.subtract).then_inc(lo_made, 1)

            def newton(v, y, t):
                order.link(dve.tensor_tensor(t, y, y, ALU.mult))
                order.link(dve.scalar_tensor_tensor(t, t, -0.5, v, ALU.mult, ALU.mult))
                order.link(dve.scalar_tensor_tensor(y, t, 1.5, y, ALU.add, ALU.mult))

            def rsqrt_steps(order, sums, scale, ready=None, apart=False):
                last = [0, 0]

                def step(i, k):
                    v, z, t = root[:, i, 0:1], rms[:, i:i + 1], root[:, i, 3:4]
                    if k == 0 and ready:
                        ready(i)
                    if k:
                        dve.wait_ge(order.sem, last[i])
                    if k == 0:
                        order.mark(dve.tensor_scalar(v, sums[i], 64.0 * scale, 64.0 * EPS, ALU.mult, ALU.add))
                    elif k == 1:
                        order.mark(dve.tensor_scalar(z.bitcast(I32), v.bitcast(I32), -0.5,
                                                     RSQRT_SEED - 2.0 ** 31, ALU.mult, ALU.add))
                    elif k % 2 == 0:
                        order.mark(dve.tensor_scalar(t, z, z, root[:, i, k // 2 - 1:k // 2], ALU.mult, ALU.mult))
                    else:
                        order.mark(dve.tensor_scalar(z, t, -3.0, z, ALU.add, ALU.mult))
                    last[i] = order.value()
                    if k == 1:
                        order.mark(dve.tensor_scalar(root[:, i, 1:2], v, 0.25, None, ALU.mult))
                        order.mark(dve.tensor_scalar(root[:, i, 2:3], v, 0.0625, None, ALU.mult))

                for k in range(4):
                    step(0, k)
                for k in range(4):
                    step(0, k + 4)
                    if not apart:
                        step(1, k)
                dve.wait_ge(order.sem, last[0])
                yield 0
                for k in range(0 if apart else 4, 8):
                    step(1, k)
                dve.wait_ge(order.sem, last[1])
                yield 1

            def norm_scale(n, between=None):
                sums = [small[:, i:i + 1] for i in range(NT)]
                ready = lambda i: dve.wait_ge(sumsq, 2 * n + i + 1)
                for i in rsqrt_steps(order, sums, 1.0 / D, ready, apart=between is not None):
                    if n < 3:
                        dve.tensor_scalar(xn_tok[:, i, :], h[:, i, :], rms[:, i:i + 1], None, ALU.mult)\
                           .then_inc(xn_ready, 1)
                    else:
                        if i == 0:
                            dve.wait_ge(wide_loaded, 32)
                        dve.scalar_tensor_tensor(xn_tok[:, i, :], h[:, i, :], rms[:, i:i + 1], g_ffn_b,
                                                 ALU.mult, ALU.mult).then_inc(xg_ready, 1)
                    if i == 0 and between:
                        between()

            def norm_lo(n, gain):
                for k in range(KD):
                    dve.wait_ge(xt_hi, 8 * n + 2 * (k // 2) + 2)
                    dve.scalar_tensor_tensor(xT_lo[:, k, :], bank[4 + k // 2][:, (k % 2) * T:(k % 2 + 1) * T],
                                             gain[:, k:k + 1], xT_hi[:, k, :], ALU.mult, ALU.subtract)\
                       .then_inc(xt_lo, 1)

            def add_to_h(i, number, last_unit):
                if i == 0:
                    dve.wait_ge(first_tile_made, number + 1)
                else:
                    dve.wait_ge(unit_used, last_unit + 1)
                for n in range(2):
                    part = h[:, i, n * 512:(n + 1) * 512]
                    ins = dve.tensor_tensor(part, bank[4 + 2 * i + n][:, :], part, ALU.add)
                    if n:
                        ins.then_inc(h_ready, 1)
                    else:
                        order.mark(ins)

            def mix(layer):
                base, heads, y0 = MIX_BASE[layer], HEADS * layer, Y_USES * layer
                uses0 = A_BASE[layer] // 2

                def used(u):
                    dve.wait_ge(unit_used, base + u + 1)

                def tap(n):
                    k, c = divmod(n, 2)
                    if n == 0:
                        dve.wait_ge(a_read[1], uses0 + 2)
                    dve.wait_ge(dve_step, order.value(0 if k == TAPS else 1))
                    if k < TAPS:
                        src, w = cin[:, c, k:k + T], pcol(layer, C_CONVW + TAPS * c + k)
                    if k == 0:
                        order.mark(dve.tensor_scalar(cacc[:, c, :], src, w, None, ALU.mult))
                    elif k < TAPS:
                        order.mark(dve.scalar_tensor_tensor(cacc[:, c, :], src, w, cacc[:, c, :],
                                                            ALU.mult, ALU.add))
                    else:
                        dve.tensor_scalar(cacc[:, c, :], cacc[:, c, :], 0.5, pcol(layer, C_CONVB + c),
                                          ALU.mult, ALU.add).then_inc(conv_v, 1)

                taps_done = 0
                for u in range(MIX_UNITS - 3):
                    for hd in range(HEADS):
                        s, two, par2 = SLOT_OF_HEAD[hd], hd % 2, 2 * (hd % 2)
                        if u == s + 2:
                            dve.wait_ge(s_exp, 2 * (heads + hd + 1))
                            order.link(dve.reciprocal(small[:, 16 + par2:18 + par2], small[:, 12 + par2:14 + par2]))
                            for q, (a, b) in enumerate(((0, 256), (256, 384))):
                                dve.tensor_scalar(S[:, two, a:b], S[:, two, a:b],
                                                  small[:, 16 + par2 + q:17 + par2 + q], None, ALU.mult)\
                                   .then_inc(p_ready, 1)
                    split_lo(base + u + AHEAD)
                    if u < 8 and u % 2:
                        c = u // 2
                        dve.wait_ge(a_read[0], uses0 + c + 1)
                        used(u)
                        dve.scalar_tensor_tensor(cin[:, c, TAPS - 1:], sig[:, c % 2, :], 1.0, bank[1][:, 0:T],
                                                 ALU.add, ALU.mult).then_inc(a_read[1], 1)
                    if u == 15:
                        for i in range(NT):
                            dve.wait_ge(y_read[i], y0 + 1)
                            order.link(dve.bn_stats(small[:, 48:54], v_tok[:, i, :]))
                            order.link(dve.bn_aggr(small[:, 28 + 2 * i:30 + 2 * i], small[:, 48:54]))
                        dve.wait_ge(sgu_par, 64 * (layer + 1))
                        var = [small[:, 29 + 2 * i:30 + 2 * i] for i in range(NT)]
                        for i in rsqrt_steps(order, var, 1.0):
                            v = v_tok[:, i, :]
                            order.link(dve.tensor_scalar(v, v, small[:, 28 + 2 * i:29 + 2 * i],
                                                         rms[:, i:i + 1], ALU.subtract, ALU.mult))
                            order.link(dve.tensor_tensor(v, v, ln_gb[:, 0, :], ALU.mult))
                            dve.tensor_tensor(v, v, ln_gb[:, 1, :], ALU.add).then_inc(vn_ready, 1)
                    if u == 19:
                        dve.wait_ge(mix_made, layer + 1)
                        for g in range(4):
                            src = bank[2 + g // 2][:, (g % 2) * T:(g % 2 + 1) * T].rearrange("p (n t) -> p n t", n=2)
                            dst = um[:, g, :].rearrange("p (n t) -> p n t", n=2)
                            ins = dve.tensor_tensor(dst, src, bs_b[:, g:g + 1, :].to_broadcast([P, 2, P]), ALU.add)
                            if g % 2:
                                ins.then_inc(y_read[g // 2], 1)
                            else:
                                order.mark(ins)
                        dve.wait_ge(y_read[1], y0 + 2)
                        dve.tensor_tensor(um, um, uT[:, :, :], ALU.mult).then_inc(um_ready, 1)
                    if u == 21:
                        dve.wait_ge(um_hi, layer + 1)
                        dve.tensor_tensor(sgu_lo, um, sgu_hi, ALU.subtract).then_inc(um_lo, 1)
                    for hd in range(HEADS):
                        s, two, par2 = SLOT_OF_HEAD[hd], hd % 2, 2 * (hd % 2)
                        if u == s:
                            dve.wait_ge(s_made, heads + hd + 1)
                            dve.wait_ge(bias_ready, layer + 1)
                            if hd >= 2:
                                dve.wait_ge(pt_made, heads + hd - 1)
                            order.mark(dve.scalar_tensor_tensor(S[:, two, 0:256], bank[4][:, 0:256], HD ** -0.5,
                                                                bias_t[:, hd, :], ALU.mult, ALU.add))
                            dve.scalar_tensor_tensor(S[:, two, 256:384], bank[4][:, 256:384], HD ** -0.5,
                                                     bias_t[:, hd, P:], ALU.mult, ALU.add).then_inc(s_read, 1)
                            dve.wait_ge(s_read, heads + hd + 1)
                            for q, (a, b) in enumerate(((0, 256), (256, 384))):
                                ins = dve.tensor_reduce(small[:, 8 + par2 + q:9 + par2 + q], S[:, two, a:b],
                                                        AX.X, ALU.max, negate=True)
                                if q:
                                    ins.then_inc(s_max, 1)
                                else:
                                    order.mark(ins)
                        if u == OUT_OF_HEAD[hd] and two:
                            dve.wait_ge(o_hi, (heads + hd + 1) // 2)
                            dve.tensor_tensor(attn_lo[:, hd // 2, :], bank[7][:, 0:T], attn_hi[:, hd // 2, :],
                                              ALU.subtract).then_inc(o_lo, 1)
                    if u >= 4 and taps_done < 2 * (TAPS + 1):
                        pace = 3 if u < 13 else 2 if u < 15 else 0 if u < 19 else 1 if u < 25 else 2
                        for _ in range(min(pace, 2 * (TAPS + 1) - taps_done)):
                            tap(taps_done)
                            taps_done += 1
                    if u == 41:
                        dve.wait_ge(mean_made, layer + 1)
                        dve.tensor_tensor(cacc[:, :, :], cacc[:, :, :],
                                          bank[5][:, 0:T].unsqueeze(1).to_broadcast([P, CG, T]),
                                          ALU.subtract).then_inc(centred, 1)
                    if u == 44:
                        dve.wait_ge(var_made, layer + 1)
                        v_st, y_st, t_st = stat[:, 0, :], stat[:, 1, :], stat[:, 2, :]
                        order.link(dve.tensor_scalar(v_st, bank[5][:, T:2 * T], EPS, None, ALU.add))
                        order.link(dve.tensor_scalar(y_st.bitcast(I32), v_st.bitcast(I32), -0.5, RSQRT_SEED,
                                                     ALU.mult, ALU.add))
                        newton(v_st, y_st, t_st)
                    if u == 45:
                        newton(v_st, y_st, t_st)
                        newton(v_st, y_st, t_st)
                        dve.tensor_tensor(cacc[:, :, :], cacc[:, :, :],
                                          stat[:, 1:2, :].to_broadcast([P, CG, T]), ALU.mult).then_inc(conv_norm, 1)
                    if u == 48:
                        dve.wait_ge(conv_act, CG * (layer + 1))
                        dve.scalar_tensor_tensor(cacc[:, :, :], csq, 1.0, cacc[:, :, :], ALU.add, ALU.mult)\
                           .then_inc(conv_y, 1)
                    if u == 50:
                        dve.wait_ge(conv_hi_s, layer + 1)
                        dve.scalar_tensor_tensor(conv_lo, cacc[:, :, :], 0.5, conv_hi, ALU.mult, ALU.subtract)\
                           .then_inc(conv_lo_s, 1)
                    for b in range(3):
                        g = u - BRANCH_UNIT[b]
                        if 0 <= g < 12 and g % 3 == 2:
                            pair, yi = g // 3, 4 * b + g // 3
                            a_uses = uses0 + 10 + 4 * b + pair + 1
                            dve.wait_ge(a_read[0], a_uses)
                            dve.wait_ge(a_read[1], a_uses)
                            used(u)
                            y = bank[2 + yi % 2][:, :].rearrange("p (m t) -> p m t", m=2)
                            dst = merged[:, 2 * pair:2 * pair + 2, :]
                            tmp = dst if b == 0 else mtmp
                            if b == 2 and pair:
                                dve.wait_ge(mrg_ready, 4 * layer + pair)
                            dve.scalar_tensor_tensor(tmp, gate_t[:, yi % 2, :, :], 1.0, y, ALU.add, ALU.mult)\
                               .then_inc(y_read[yi % 2], 1)
                            if b:
                                dve.wait_ge(y_read[yi % 2], y0 + 3 + yi // 2 + 1)
                                ins = dve.tensor_tensor(dst, dst, tmp, ALU.add)
                                if b == 2:
                                    ins.then_inc(mrg_ready, 1)
                                else:
                                    order.link(ins)
                    if u >= BRANCH_UNIT[2] + 3 and (u - BRANCH_UNIT[2]) % 3 == 0 and u <= 64:
                        pair = (u - BRANCH_UNIT[2]) // 3 - 1
                        merged_lo(layer, pair)

            def after_mix(layer):
                last_unit = MIX_BASE[layer] + MIX_UNITS - 1

                def tile_1():
                    add_to_h(1, 2 * layer, last_unit)
                    split_lo(last_unit + 3)

                add_to_h(0, 2 * layer, last_unit)
                norm_scale(2 * layer + 1, tile_1)

            def late_splits(layer):
                for u in range(2):
                    split_lo(MIX_BASE[layer] + MIX_UNITS + 3 + u)

            def merged_lo(layer, pair):
                dve.wait_ge(mrg_hi_s, 4 * layer + pair + 1)
                dve.scalar_tensor_tensor(mrg_lo[:, 2 * pair:2 * pair + 2, :], merged[:, 2 * pair:2 * pair + 2, :],
                                         0.5, mrg_hi[:, 2 * pair:2 * pair + 2, :], ALU.mult, ALU.subtract)\
                   .then_inc(mrg_lo_s, 1)

            def ffn_mul(f, turn=None):
                u = FFN_BASE + (2 + 3 * (f - 1) if f else 0) + 1
                dve.wait_ge(unit_used, at(u + 1, turn, 12))
                dve.wait_ge(a_read[0], at(FFN_A_BASE // 2 + f + 1, turn, 4))
                dve.tensor_tensor(f_h[:, f % 2, :], f_sl[:, f % 2, :], bank[1][:, 0:T], ALU.mult)\
                   .then_inc(a_read[1], 1)

            def ffn_lo(f, turn=None):
                dve.wait_ge(fh_hi_s, at(f + 1, turn, 4))
                dve.tensor_tensor(fh_lo[:, f % 2, :], f_h[:, f % 2, :], fh_hi[:, f % 2, :], ALU.subtract)\
                   .then_inc(fh_lo_s, 1)

            def ffn_step(f, turn=None):
                u = FFN_BASE + 2 + 3 * (f - 1)
                split_lo(u + AHEAD, turn)
                split_lo(u + 1 + AHEAD, turn)
                ffn_mul(f, turn)
                split_lo(u + 2 + AHEAD, turn)
                ffn_lo(f, turn)

            def build_pick(n, e=None):
                if n:
                    dve.wait_ge(pickT_made, at(n, e, 1))
                for i in range(NT):
                    c = bass.ds(at(0 if e is None else 1, e, 1), 1)
                    ins = dve.tensor_scalar(pick[:, i, :], iota, slot[:, i, c], chosen[:, i, c],
                                            ALU.is_equal, ALU.mult)
                    ins.then_inc(pick_ready, 1)

            def gather_read(n, e=None, rounds=(1, 3)):
                for r in rounds:
                    dve.wait_ge(gathered, at(4 * n + r + 1, e, 4))
                    dve.tensor_copy(slot_parts[r // 2][:, 4:8, :],
                                    bank[6][:, :].rearrange("p (k s) -> p k s", k=4)).then_inc(slots_v, 1)

            def expert_lo(rnd, e, j, dst=eh_lo, hi=eh_hi):
                dve.wait_ge(eh_hi_s, at(NJ * NE * rnd + j + 1, e, NJ))
                dve.tensor_tensor(dst, bank[2][:, :].rearrange("p (k s) -> p k s", k=4), hi,
                                  ALU.subtract).then_inc(eh_lo_s, 1)

            def spread_add(n, q, e):
                i, half = divmod(q, 2)
                dve.wait_ge(spread, at(4 * n + q + 1, e, 4))
                part = h[:, i, half * 512:(half + 1) * 512]
                c = bass.ds(at(0, e, 1), 1)
                dve.scalar_tensor_tensor(part, bank[6 + q % 2][:, :], weight[:, i, c], part,
                                         ALU.mult, ALU.add).then_inc(spread_read, 1)

            def expert(rnd, e, last=False):
                u0 = MOE_BASE + MOE_UNITS * NE * rnd
                for k in range(MOE_UNITS):
                    if not last or k + AHEAD < MOE_UNITS:
                        split_lo(u0 + k + AHEAD, e, MOE_UNITS)
                    j, q = (0, k) if k < 8 else ((k - 8) // 12 + 1, (k - 8) % 12)
                    if j == 0 and q in (4, 5):
                        spread_add(NE * rnd, q - 4, e)
                    if j == 1 and q in (0, 1):
                        spread_add(NE * rnd, q + 2, e)
                    if 0 < j < NJ and q == 2:
                        expert_lo(rnd, e, j - 1)
                    if j < NJ and q == 7:
                        c = NJ * NE * rnd + j
                        dve.wait_ge(unit_used, at(u0 + k + 1, e, MOE_UNITS))
                        dve.wait_ge(a_read[0], at(MOE_A_USES + c + 1, e, NJ))
                        dve.tensor_tensor(e_h, e_sl, bank[1][:, :], ALU.mult).then_inc(a_read[1], 1)
                    if j == 2 and q == 0 and not last:
                        build_pick(NE * rnd + 1, e)
                    if j == NJ - 1 and q == 7:
                        if not last:
                            gather_read(NE * rnd + 1, e, (1,))
                            expert_lo(rnd, e, NJ - 1)
                            gather_read(NE * rnd + 1, e, (3,))
                    if j == NJ - 1 and q == 9 and last:
                        expert_lo(rnd, e, NJ - 1, eh2_lo, eh2_hi)
                for n in range(2):
                    dve.wait_ge(ye_hi_s, at(2 * NE * rnd + n + 1, e, 2))
                    part = slice(n * 512, (n + 1) * 512)
                    dve.tensor_tensor(ye_lo[:, part], bank[4 + n][:, :], ye_hi[:, part], ALU.subtract)\
                       .then_inc(ye_lo_s, 1)

            order.mark(dve.memset(cin[:, :, 0:TAPS - 1], 0.0))
            order.mark(dve.memset(chosen[:, :, :], 0.0))
            order.mark(dve.memset(weight[:, :, :], 0.0))
            order.mark(dve.memset(rank[:, :, :], 0.0))
            norm_scale(0)
            split_lo(0)
            dve.wait_ge(par_loaded, 16)
            norm_lo(0, pcol(0, C_MIXG, 8))
            for u in range(1, AHEAD):
                split_lo(u)
            dve.tensor_scalar(par_half[:, :], par[:, :], 0.5, None, ALU.mult).then_inc(par_ready, 1)
            mix(0)
            after_mix(0)
            norm_lo(1, pcol(0, C_FFNG, 8))
            late_splits(0)
            split_lo(FFN_BASE + AHEAD)
            split_lo(FFN_BASE + 1 + AHEAD)
            ffn_mul(0)
            ffn_lo(0)
            with dve.Fori(0, 5) as turn:
                for f in range(1, 5):
                    ffn_step(f, turn)
            ffn_step(FT - 1)
            split_lo(FFN_BASE + FFN_UNITS - 1 + AHEAD)
            for i in range(NT):
                add_to_h(i, 1, FFN_BASE + FFN_UNITS - 1)
            norm_scale(2)
            norm_lo(2, pcol(1, C_MIXG, 8))
            mix(1)
            after_mix(1)

            for i in range(NT):
                dve.wait_ge(tok_hi_s, i + 1)
                dve.tensor_tensor(tok_lo[:, i, :], xn_tok[:, i, :], tok_hi[:, i, :], ALU.subtract)\
                   .then_inc(tok_lo_s, 1)
            dve.memset(br_ab[:, 2048:4096].bitcast(F32), 0.0).then_inc(ye_lo_s, 1)
            dve.memset(pickT.bitcast(F32), 0.0).then_inc(pickT_read, 1)
            dve.wait_ge(route_const, 2)
            dve.wait_ge(logitsT_made, 1)
            dve.tensor_copy(logitsT, bank[3][0:NE, 0:T]).then_inc(logitsT_read, 1)
            dve.wait_ge(logits_made, 1)
            logit = [bank[2][:, NE * i:NE * (i + 1)] for i in range(NT)]
            for i in range(NT):
                order.mark(dve.max(top[:, i, :], logit[i]))
            for i in range(NT):
                dve.wait_ge(dve_step, order.value(1))
                order.mark(dve.max_index(topi[:, i, :], top[:, i, :], logit[i]))
            dve.tensor_tensor(small[:, 20:22], top[:, :, 1], top[:, :, 0], ALU.subtract).then_inc(gap_ready, 1)
            dve.wait_ge(dve_step, order.value())
            order.link(dve.tensor_copy(best, topi[:, :, 0:2]))
            wide = [P, NT, 2, NE]
            order.link(dve.tensor_tensor(sel[:, :, :, :], iota[:, 0:NE].unsqueeze(1).unsqueeze(1).to_broadcast(wide),
                                         best.unsqueeze(3).to_broadcast(wide), ALU.is_equal))
            dve.tensor_tensor(chosen[:, :, 0:NE], sel[:, :, 0, :], sel[:, :, 1, :], ALU.add).then_inc(chosen_ready, 1)
            dve.wait_ge(gap_exp, 1)
            order.link(dve.tensor_scalar(small[:, 26:28], small[:, 24:26], 1.0, None, ALU.add))
            order.link(dve.reciprocal(share[:, :, 0], small[:, 26:28]))
            order.link(dve.tensor_tensor(share[:, :, 1], small[:, 24:26], share[:, :, 0], ALU.mult))
            order.link(dve.tensor_tensor(sel[:, :, :, :], sel[:, :, :, :], share.unsqueeze(3).to_broadcast(wide), ALU.mult))
            order.mark(dve.tensor_tensor(weight[:, :, 1:NE + 1], sel[:, :, 0, :], sel[:, :, 1, :], ALU.add))
            dve.wait_ge(rank_made, 1)
            dve.tensor_copy(rank[:, :, 0:NE], bank[2][:, 16:32].rearrange("p (i e) -> p i e", i=2))\
               .then_inc(rank_read, 1)
            dve.wait_ge(rank_read, 1)

            def experts(rnd):
                order.link(dve.tensor_scalar(slot[:, :, :], rank[:, :, :], float(-P * rnd), None, ALU.add))
                build_pick(NE * rnd)
                if rnd == 0:
                    late_splits(1)
                    dve.wait_ge(total_made, 1)
                    order.link(dve.tensor_reduce(small[:, 44:45], bank[2][:, 32:40], AX.X, ALU.max))
                    order.link(dve.tensor_scalar(small[:, 45:46], small[:, 44:45], float(P), None, ALU.is_gt))
                    dve.tensor_copy(flag[:, :], small[:, 45:46]).then_inc(flag_ready, 1)
                gather_read(NE * rnd)
                with dve.Fori(0, NE - 1) as e:
                    expert(rnd, e)
                expert(rnd, NE - 1, last=True)

            experts(0)
            dve.wait_ge(flag_ready, 1)
            again = dve.value_load(flag[0:1, 0:1], min_val=0, max_val=1)
            with dve.If(again > 0):
                order.link(dve.tensor_copy(weight[:, :, 0:1], weight[:, :, NE:NE + 1]))
                for u in range(AHEAD):
                    split_lo(MOE_BASE + MOE_UNITS * NE + u)
                experts(1)
            for q in range(4):
                i, half = divmod(q, 2)
                dve.wait_ge(last_spread, q + 1)
                part = h[:, i, half * 512:(half + 1) * 512]
                ins = dve.scalar_tensor_tensor(part, bank[6 + q % 2][:, :], weight[:, i, NE:NE + 1], part,
                                               ALU.mult, ALU.add)
                ins.then_inc(last_spread_read, 1)
            last = Order(dve, final_step)
            sums = [small[:, i:i + 1] for i in range(NT)]
            for i in rsqrt_steps(last, sums, 1.0 / D, lambda i: dve.wait_ge(sumsq, 2 * 4 + i + 1)):
                dve.memset(small[:, 60 + i:61 + i], 0.0).then_inc(rms_ready, 1)
            dve.wait_ge(gained, 2)
            for half in range(2):
                c = slice(half * 512, (half + 1) * 512)
                dve.tensor_scalar(xn_tok[:, 1, c], xn_tok[:, 1, c], rms[:, 1:2], None, ALU.mult)\
                   .then_inc(out_ready[1], 1)

        @block.tensor
        def _(pe):
            def unit(u, view, turn=None, stride=12):
                pe.wait_ge(lo_made, at(u + 1, turn, stride))
                return [w[:, u % SPLIT, :].rearrange("p (k n) -> p k n", k=view) for w in (whi, wlo)]

            def product(out_ap, a, b, first, last):
                pe.matmul(out_ap, a[0], b[0], start=first, stop=False)
                pe.matmul(out_ap, a[0], b[1], start=False, stop=False)
                return pe.matmul(out_ap, a[1], b[0], start=False, stop=last)

            def turned(out_ap, w, c, rhs, k_tiles):
                for k in range(k_tiles):
                    ins = product(out_ap, [w[0][:, k, c:c + P], w[1][:, k, c:c + P]],
                                  [rhs[0][:, k, :], rhs[1][:, k, :]], k == 0, k == k_tiles - 1)
                return ins

            def first_product(out_ap, w, norm):
                for k in range(KD):
                    pe.wait_ge(xt_lo, KD * norm + k + 1)
                    ins = product(out_ap, [w[0][:, k, :], w[1][:, k, :]], [xT_hi[:, k, :], xT_lo[:, k, :]],
                                  k == 0, k == KD - 1)
                return ins

            def norm_turn(n):
                if n:
                    pe.wait_ge(a_read[0], [0, MIX_A // 2, (MIX_A + FFN_A) // 2, MOE_A_USES][n])
                if n == 2:
                    keep_warm(16)
                for i in range(NT):
                    if n < 3:
                        pe.wait_ge(xn_ready, 2 * n + i + 1)
                    else:
                        pe.wait_ge(xg_ready, i + 1)
                    for k in range(KD):
                        if n % 2 and i == 0 and k == 4:
                            keep_warm(6)
                            pe.wait_ge(h_ready, 2 * n)
                        dst = bank[4 + k // 2][:, (k % 2) * T + i * P:(k % 2) * T + (i + 1) * P]
                        ins = pe.transpose(dst, xn_tok[:, i, k * P:(k + 1) * P], ident[:, :])
                        if i and k % 2:
                            ins.then_inc(xt_made, 1)
                    if i == 0:
                        keep_warm((2, 10, 2, 12)[n])

            def mix(layer):
                base, heads, y0 = MIX_BASE[layer], HEADS * layer, Y_USES * layer
                uses0 = A_BASE[layer] // 2
                norm = 2 * layer
                xs = [xT_hi, xT_lo]
                a_index = 0

                def a_unit(u):
                    nonlocal a_index
                    b = a_index % 2
                    w = unit(base + u, KD)
                    if uses0 + a_index // 2:
                        pe.wait_ge(a_read[b], uses0 + a_index // 2)
                    if a_index == 0:
                        ins = first_product(bank[b][:, 0:T], w, norm)
                    else:
                        ins = turned(bank[b][:, 0:T], w, 0, xs, KD)
                    ins.then_inc(unit_used, 1)
                    a_index += 1

                def v_units(u, use):
                    if y0 + use:
                        for i in range(NT):
                            pe.wait_ge(y_read[i], y0 + use)
                    for n in range(4):
                        w = unit(base + u + n, 2)
                        for i in range(NT):
                            for k in range(2):
                                kk = 2 * n + k
                                t = slice(i * P, (i + 1) * P)
                                ins = product(bank[2 + i][:, :], [xT_hi[:, kk, t], xT_lo[:, kk, t]],
                                              [w[0][:, k, :], w[1][:, k, :]], kk == 0, kk == KD - 1)
                        ins.then_inc(unit_used, 1)
                        extras(u + n)

                def y_unit(u, b, pair):
                    yi = 4 * b + pair
                    w = unit(base + u, 4)
                    pe.wait_ge([um_lo, o_lo, conv_lo_s][b], [layer + 1, 4 * layer + 4, layer + 1][b])
                    pe.wait_ge(y_read[yi % 2], y0 + 3 + yi // 2)
                    for m in range(2):
                        ins = turned(bank[2 + yi % 2][:, m * T:(m + 1) * T], w, m * P, branch_parts[b], 4)
                    ins.then_inc(unit_used, 1)

                def sgu_mix():
                    pe.wait_ge(vn_ready, 2 * layer + 2)
                    pe.wait_ge(sgu_mask, layer + 1)
                    for i in range(NT):
                        pe.wait_ge(y_read[i], y0 + 1)
                    for g in range(4):
                        for n in range(NT):
                            c = (g % 2) * T + n * P
                            ins = pe.matmul(bank[2 + g // 2][:, c:c + P], v_tok[:, n, g * P:(g + 1) * P],
                                            wsT[:, g, :], start=True, stop=True)
                    ins.then_inc(mix_made, 1)

                def scores(hd):
                    r, i = slice(64 * (hd % 2), 64 * (hd % 2) + 64), hd // 2
                    if r.start == 0:
                        pe.wait_ge(a_read[0], uses0 + 7 + i)
                        pe.wait_ge(a_read[1], uses0 + 7 + i)
                    if heads + hd:
                        pe.wait_ge(s_read, heads + hd)
                    pe.matmul(bank[4][:, 0:256], qT[r, i, P:T], kT[r, i, :], start=True, stop=True)
                    pe.matmul(bank[4][:, 256:384], qT[r, i, 0:P], kT[r, i, 0:P], start=True, stop=True)\
                      .then_inc(s_made, 1)

                def turn_p(hd):
                    pe.wait_ge(p_ready, 2 * (heads + hd + 1))
                    if heads + hd:
                        pe.wait_ge(pt_read, heads + hd)
                    for n, c in enumerate((256, 0, 128)):
                        ins = pe.transpose(bank[6][:, n * P:(n + 1) * P], S[:, hd % 2, c:c + P], ident[:, :])
                    ins.then_inc(pt_made, 1)

                def head_out(hd):
                    r = slice(64 * (hd % 2), 64 * (hd % 2) + 64)
                    pe.wait_ge(pt_read, heads + hd + 1)
                    pe.wait_ge(y_read[1], y0 + 3)
                    if heads + hd > 1:
                        pe.wait_ge(o_lo, (heads + hd) // 2)
                    c = slice(hd * HD, (hd + 1) * HD)
                    pe.matmul(bank[7][r, 0:T], v_att[:, 0, c], pT[:, hd % 2, 0:T], start=True, stop=False)
                    pe.matmul(bank[7][r, P:T], v_att[:, 1, c], pT[:, hd % 2, T:384], start=False, stop=True)\
                      .then_inc(o_made, 1)

                def channel_mean(n):
                    pe.wait_ge(tiles_summed, 2 * layer + n + 1)
                    return pe.matmul(bank[5][:, n * T:(n + 1) * T], ones[:, :], tile_sum, start=True, stop=True)

                def extras(u):
                    if u == 19:
                        sgu_mix()
                    if u == 41:
                        channel_mean(0).then_inc(mean_made, 1)
                    if u == 44:
                        channel_mean(1).then_inc(var_made, 1)
                    for hd in range(HEADS):
                        if u == SLOT_OF_HEAD[hd]:
                            scores(hd)
                        if u == SLOT_OF_HEAD[hd] + 3:
                            turn_p(hd)
                        if u == OUT_OF_HEAD[hd]:
                            head_out(hd)

                for u in range(12):
                    a_unit(u)
                v_units(12, 0)
                for u in range(16, 24):
                    a_unit(u)
                    extras(u)
                v_units(24, 2)
                for b in range(3):
                    for pair in range(4):
                        u = BRANCH_UNIT[b] + 3 * pair
                        for m in range(2):
                            a_unit(u + m)
                            extras(u + m)
                        y_unit(u + 2, b, pair)
                        extras(u + 2)
                for k in range(4):
                    w = unit(base + 64 + k, 1)
                    pe.wait_ge(mrg_lo_s, 4 * layer + k // 2 + 1)
                    by_token(k, w, [mrg_hi, mrg_lo], k == 0, False).then_inc(unit_used, 1)
                for i in range(NT):
                    for k in range(4, KD):
                        w = unit(base + 64 + k, 1)
                        pe.wait_ge(mrg_lo_s, 4 * layer + k // 2 + 1)
                        ins = by_token(k, w, [mrg_hi, mrg_lo], False, k == KD - 1, tiles=(i,))
                        if i:
                            ins.then_inc(unit_used, 1)

            def by_token(k, w, parts, first, last, tiles=(0, 1)):
                for i in tiles:
                    t = slice(i * P, (i + 1) * P)
                    for n in range(2):
                        c = slice(n * 512, (n + 1) * 512)
                        ins = product(bank[4 + 2 * i + n][:, :], [parts[0][:, k, t], parts[1][:, k, t]],
                                      [w[0][:, 0, c], w[1][:, 0, c]], first, last)
                    if last and i == 0:
                        ins.then_inc(first_tile_made, 1)
                return ins

            def ffn_up(f, turn=None):
                u = FFN_BASE + (2 + 3 * (f - 1) if f else 0)
                for b in range(2):
                    w = unit(u + b, KD, turn)
                    pe.wait_ge(a_read[b], at(FFN_A_BASE // 2 + f, turn, 4))
                    if f == 0 and b == 0:
                        ins = first_product(bank[b][:, 0:T], w, 1)
                    else:
                        ins = turned(bank[b][:, 0:T], w, 0, [xT_hi, xT_lo], KD)
                    ins.then_inc(unit_used, 1)

            def ffn_down(f, u, turn=None, first=False, last=False):
                w = unit(u, 1, turn)
                pe.wait_ge(fh_lo_s, at(f + 1, turn, 4))
                by_token(f % 2, w, [fh_hi, fh_lo], first, last).then_inc(unit_used, 1)

            def ffn_step(f, turn=None, first=False):
                ffn_up(f, turn)
                ffn_down(f - 1, FFN_BASE + 2 + 3 * (f - 1) + 2, turn, first)

            def gather(n, e, rounds):
                for r in rounds:
                    pe.wait_ge(pick_ready, at(2 * n + 2, e, 2))
                    if r % 2 == 0 and (n or e is not None or r):
                        pe.wait_ge(slots_a, at(2 * n + r // 2, e, 2))
                    if r % 2 == 1 and (n or e is not None or r > 1):
                        pe.wait_ge(slots_v, at(2 * n + r // 2, e, 2))
                    src, b = (tok_hi, tok_lo)[r // 2], bank[3] if r % 2 == 0 else bank[6]
                    for q in range(4):
                        k = 4 * (r % 2) + q
                        for i in range(NT):
                            ins = pe.matmul(b[:, q * P:(q + 1) * P], src[:, i, k * P:(k + 1) * P],
                                            pick[:, i, :], start=i == 0, stop=i == NT - 1)
                    ins.then_inc(gathered, 1)

            def spread_round(n, q, e=None, done=(spread, spread_read)):
                i, half = divmod(q, 2)
                c = slice(half * 512, (half + 1) * 512)
                if q >= 2:
                    pe.wait_ge(done[1], at(4 * n + q - 1, e, 4))
                for s, y in enumerate((ye_hi, ye_lo)):
                    ins = pe.matmul(bank[6 + q % 2][:, :], pickT[:, i * P:(i + 1) * P], y[:, c],
                                    start=s == 0, stop=s == 1)
                ins.then_inc(done[0], 1)

            def expert(rnd, e, last=False):
                u = MOE_BASE + MOE_UNITS * NE * rnd

                def take(view):
                    nonlocal u
                    u += 1
                    return unit(u - 1, view, e, MOE_UNITS)

                def turn_hidden(j):
                    pe.wait_ge(a_read[1], at(MOE_A_USES + NJ * NE * rnd + j + 1, e, NJ))
                    for k in range(4):
                        ins = pe.transpose(bank[2][:, k * P:(k + 1) * P], e_h[:, k * P:(k + 1) * P], ident[:, :])
                    ins.then_inc(eh_made, 1)

                def down(j):
                    hi, lo = (eh2_hi, eh2_lo) if last and j == NJ - 1 else (eh_hi, eh_lo)
                    for k in range(4):
                        if last and j == NJ - 2 and k == 2:
                            turn_hidden(NJ - 1)
                        w = take(1)
                        if k == 0:
                            pe.wait_ge(eh_lo_s, at(NJ * NE * rnd + j + 1, e, NJ))
                        for n in range(2):
                            c = slice(n * 512, (n + 1) * 512)
                            ins = product(bank[4 + n][:, :], [hi[:, k, :], lo[:, k, :]],
                                          [w[0][:, 0, c], w[1][:, 0, c]], j == 0 and k == 0, j == NJ - 1 and k == 3)
                            if j == NJ - 1 and k == 3 and n == 0:
                                ins.then_inc(y_half_made, 1)
                        ins.then_inc(unit_used, 1)

                pe.wait_ge(slots_a, at(2 * NE * rnd + 2, e, 2))
                for j in range(NJ):
                    for b in range(2):
                        pe.wait_ge(a_read[b], at(MOE_A_USES + NJ * NE * rnd + j, e, NJ))
                        for q in range(4):
                            if j == b == 0 and q == 2:
                                pe.wait_ge(slots_v, at(2 * NE * rnd + 2, e, 2))
                            w = take(2)
                            for k in range(2):
                                kk = 2 * q + k
                                ins = product(bank[b][:, :], [p[:, kk, :] for p in slot_parts],
                                              [w[0][:, k, :], w[1][:, k, :]], kk == 0, kk == KD - 1)
                            ins.then_inc(unit_used, 1)
                            if b == 0 and q == 0 and j:
                                turn_hidden(j - 1)
                        if j == 0:
                            if b == 0:
                                pe.wait_ge(ye_lo_s, at(2 * NE * rnd + 1, e, 2))
                                pe.wait_ge(pickT_read, at(NE * rnd + 1, e, 1))
                            spread_round(NE * rnd, 2 * b, e)
                            spread_round(NE * rnd, 2 * b + 1, e)
                    if j == 1:
                        pe.wait_ge(spread_read, at(4 * NE * rnd + 4, e, 4))
                        for i in range(NT):
                            ins = pe.transpose(bank[7][:, i * P:(i + 1) * P], pick[:, i, :].bitcast(F32), ident[:, :])
                        ins.then_inc(pickT_made, 1)
                    if j == NJ - 1 and not last:
                        gather(NE * rnd + 1, e, (0, 1))
                    if j:
                        down(j - 1)
                if not last:
                    turn_hidden(NJ - 1)
                    gather(NE * rnd + 1, e, (2, 3))
                down(NJ - 1)

            def keep_warm(n):
                for _ in range(n):
                    pe.matmul(bank[0][:, 0:P], ident[:, :], ident[:, :], start=True, stop=True)

            pe.wait_ge(consts, 2)
            keep_warm(10)
            norm_turn(0)
            mix(0)
            norm_turn(1)
            ffn_up(0)
            ffn_up(1)
            ffn_down(0, FFN_BASE + 4, first=True)
            with pe.Fori(0, 5) as turn:
                for f in range(2, 6):
                    ffn_step(f, turn)
            ffn_down(FT - 1, FFN_BASE + FFN_UNITS - 1, last=True)
            norm_turn(2)
            mix(1)
            norm_turn(3)
            keep_warm(2)
            pe.wait_ge(router_in, 16)
            pe.wait_ge(route_const, 2)
            for i in range(NT):
                pe.wait_ge(y_read[i], 2 * Y_USES)
            for k in range(KD):
                pe.wait_ge(route_read, k // 2 + 1)
                ins = pe.matmul(bank[3][0:NE, 0:T], router[:, k, :], routeT[:, k, :], start=k == 0, stop=k == KD - 1)
            ins.then_inc(logitsT_made, 1)
            keep_warm(2)
            pe.wait_ge(logitsT_read, 1)
            for i in range(NT):
                ins = pe.transpose(bank[2][:, NE * i:NE * (i + 1)], logitsT[:, i * P:(i + 1) * P], ident[0:NE, 0:NE])
            ins.then_inc(logits_made, 1)
            keep_warm(5)
            pe.wait_ge(chosen_ready, 1)
            pe.matmul(bank[2][:, 16:24], upper, chosen[:, 0, 0:NE], start=True, stop=True)
            pe.matmul(bank[2][:, 24:32], ones1, chosen[:, 0, 0:NE], start=True, stop=False)
            pe.matmul(bank[2][:, 24:32], upper, chosen[:, 1, 0:NE], start=False, stop=True).then_inc(rank_made, 1)
            pe.wait_ge(rank_read, 1)
            pe.matmul(bank[2][:, 32:40], ones1, chosen[:, 0, 0:NE], start=True, stop=False)
            pe.matmul(bank[2][:, 32:40], ones1, chosen[:, 1, 0:NE], start=False, stop=True).then_inc(total_made, 1)
            keep_warm(6)
            pe.wait_ge(tok_lo_s, 2)

            def experts(rnd):
                if rnd:
                    pe.wait_ge(spread_read, 4 * NE * rnd)
                gather(NE * rnd, None, range(4))
                pe.wait_ge(flag_ready, 1)
                with pe.Fori(0, NE - 1) as e:
                    expert(rnd, e)
                expert(rnd, NE - 1, last=True)

            experts(0)
            again = pe.value_load(flag[0:1, 0:1], min_val=0, max_val=1)
            with pe.If(again > 0):
                experts(1)
                pe.wait_ge(ye_lo_s, 2 * NE * 2 + 1)
                pe.wait_ge(pickT_read, NE * 2 + 1)
            pe.wait_ge(pickT_read, NE + 1)
            for q in range(4):
                pe.wait_ge(ye_lo_s, 2 * NE + q % 2)
                spread_round(0, q, done=(last_spread, last_spread_read))

        @block.gpsimd
        def _(pool):
            order = Order(pool, pool_step)
            pool.dma_start(par[:, :], params).then_inc(par_loaded, 16)
            pool.dma_start(extv[:, 127:127 + N_REL], rel_reversed).then_inc(rel_in, 16)
            order.mark(pool.memset(ident[:, :], 0.0))
            pool.memset(ones[:, :], 1.0 / CW).then_inc(consts, 1)
            pool.wait_ge(pool_step, 1)
            pool.affine_select(out=ident[:, :], in_=ident[:, :], compare_op=ALU.not_equal, fill=1.0,
                               base=0, pattern=[[-1, P]], channel_multiplier=1).then_inc(consts, 1)
            pool.wait_ge(rel_in, 16)
            order.mark(pool.tensor_copy(extv[:, 0:127], extv[:, 127:128].to_broadcast([L * HEADS, 127])))
            order.link(pool.tensor_copy(extv[:, 319:384], extv[:, 318:319].to_broadcast([L * HEADS, 65])))
            pool.dma_start(scratch, extv[:, 0:384].unsqueeze(1).to_broadcast([L * HEADS, P, 384])).then_inc(rel_out, 16)

            def load_params(layer):
                pool.dma_start(ln_gb[:, 0, :], sgu_ln_g[layer:layer + 1, :].partition_broadcast(P)).then_inc(sgu_par, 16)
                pool.dma_start(ln_gb[:, 1, :], sgu_ln_b[layer:layer + 1, :].partition_broadcast(P)).then_inc(sgu_par, 16)
                pool.dma_start(bs_b[:, :, :], sgu_bs[layer].partition_broadcast(P)).then_inc(sgu_par, 16)
                pool.dma_start(wsT[:, :, :], sgu_wsT[layer]).then_inc(sgu_par, 16)

            def load_bias(layer):
                pool.wait_ge(rel_out, 16)
                rows = scratch[layer * HEADS:(layer + 1) * HEADS]
                pool.dma_start(bias_t[:, :, :], bass.AP(rows.tensor, rows.offset + P - 1,
                                                        [[383, P], [P * 384, HEADS], [1, 2 * P]])).then_inc(bias_in, 16)

            def mask_mixing(layer):
                pool.wait_ge(sgu_par, 64 * (layer + 1))
                pool.memset(wsT[64:128, :, 0:64], 0.0).then_inc(sgu_mask, 1)
                pool.wait_ge(sgu_mask, layer + 1)

            def mask_bias(layer):
                pool.wait_ge(bias_in, 16 * (layer + 1))
                pool.memset(bias_t[0:64, :, 192:256], NEG).then_inc(bias_ready, 1)
                pool.wait_ge(bias_ready, layer + 1)

            def conv_taps(layer):
                for k in range(1, TAPS):
                    if k == 2:
                        load_bias(layer)
                    if k in (7, 12):
                        pool.wait_ge(tap_added, (TAPS - 1) * layer + k - 1)
                        if k == 7:
                            mask_mixing(layer)
                        else:
                            mask_bias(layer)
                    pool.wait_ge(tap_made, 2 * (TAPS * layer + k + 1))
                    if k > 1:
                        pool.wait_ge(tap_added, (TAPS - 1) * layer + k - 1)
                    pool.tensor_tensor(cacc[:, 2:4, :], cacc[:, 2:4, :], tap_prod[:, k % 2, :, :], ALU.add)\
                        .then_inc(tap_added, 1)
                pool.wait_ge(tap_added, (TAPS - 1) * (layer + 1))
                pool.wait_ge(par_loaded, 16)
                for c in (2, 3):
                    pool.tensor_scalar(cacc[:, c, :], cacc[:, c, :], 0.5, pcol(layer, C_CONVB + c),
                                       ALU.mult, ALU.add).then_inc(conv_p, 1)
                pool.wait_ge(conv_p, 2 * (layer + 1))
                pool.wait_ge(conv_v, 2 * (layer + 1))
                for n, src in enumerate((cacc, csq)):
                    if n:
                        pool.wait_ge(squared, layer + 1)
                    order.link(pool.tensor_tensor(stat[:, 2:4, :], src[:, 0:2, :], src[:, 2:4, :], ALU.add))
                    pool.tensor_tensor(tile_sum, stat[:, 2, :], stat[:, 3, :], ALU.add).then_inc(tiles_summed, 1)
                    pool.wait_ge(tiles_summed, 2 * layer + n + 1)

            load_params(0)
            conv_taps(0)
            pool.wait_ge(um_lo, 1)
            pool.wait_ge(o_lo, 4)
            load_params(1)
            conv_taps(1)
            pool.wait_ge(mrg_ready, 4 * L)
            pool.dma_start(g_ffn_b, ffn_norm_g[1:2, :].partition_broadcast(P)).then_inc(wide_loaded, 16)
            pool.dma_start(g_fin_b, final_norm_g.unsqueeze(0).partition_broadcast(P)).then_inc(wide_loaded, 16)
            pool.dma_start(router, moe_router[0].rearrange("(k p) e -> p k e", p=P)).then_inc(router_in, 16)
            order.mark(pool.iota(iota_i[:, :], [[1, P]], base=0, channel_multiplier=0))
            order.link(pool.memset(ones1, 1.0))
            pool.affine_select(out=upper, in_=ones1, compare_op=ALU.is_gt, fill=0.0,
                               base=0, pattern=[[1, P]], channel_multiplier=-1).then_inc(route_const, 1)
            pool.tensor_copy(iota, iota_i[:, :]).then_inc(route_const, 1)

            pool.wait_ge(route_const, 2)
            pool.wait_ge(wide_loaded, 32)
            for i in range(NT):
                pool.wait_ge(last_spread_read, 2 * i + 2)
                pool.tensor_tensor(xn_tok[:, i, :], h[:, i, :], g_fin_b, ALU.mult).then_inc(gained, 1)
                pool.wait_ge(gained, i + 1)


_OUTS = [((1, 256, 1024), "float32")]


def kernel(**inputs):
    import numpy as _np
    import concourse.bacc as _bacc
    from concourse import mybir as _mybir
    from concourse.bass_utils import run_bass_kernel_spmd as _run

    a = {k: _np.asarray(v) for k, v in inputs.items()}

    def columns(v):
        return v.reshape(-1, P).T

    par = []
    for layer in range(L):
        taps = a["conv_dw_w"][layer].reshape(TAPS, CG, P).transpose(2, 1, 0).reshape(P, CG * TAPS)
        par += [columns(a["mix_norm_g"][layer]), columns(a["b_gate"][layer]), taps,
                columns(a["conv_dw_b"][layer]), columns(a["conv_ln_g"][layer]),
                columns(a["conv_ln_b"][layer]), columns(a["ffn_norm_g"][layer])]
    feed = {k: a[k] for k in ("x", "w_in", "conv_out_w", "sgu_out_w", "attn_out_w", "w_out", "ffn_w_gate",
                              "ffn_w_up", "ffn_w_down", "moe_router", "moe_w_gate", "moe_w_up", "moe_w_down")}
    feed["params"] = _np.concatenate(par, axis=1)
    feed["sgu_ln_g"], feed["sgu_ln_b"] = a["sgu_ln_g"], a["sgu_ln_b"]
    feed["sgu_wsT"] = a["sgu_ws"].transpose(0, 3, 1, 2)
    feed["sgu_bs"] = a["sgu_bs"]
    feed["rel_reversed"] = a["attn_rel_bias"][:, :, ::-1].reshape(L * HEADS, N_REL)
    feed["ffn_norm_g"], feed["final_norm_g"] = a["ffn_norm_g"], a["final_norm_g"]

    nc = _bacc.Bacc("TRN2", target_bir_lowering=False, num_devices=1)
    arrays, args = {}, []
    for name, v in feed.items():
        v = _np.ascontiguousarray(v)
        arrays[f"in_{name}_dram"] = v
        args.append(nc.dram_tensor(f"in_{name}_dram", v.shape, _mybir.dt.from_np(v.dtype), kind="ExternalInput").ap())
    for i, (shape, dtype) in enumerate(_OUTS):
        dt = _mybir.dt.from_np(_np.dtype(dtype))
        args.append(nc.dram_tensor(f"out_{i}_dram", shape, dt, kind="ExternalOutput").ap())
    trunk(nc, *args)
    r = _run(nc, [arrays], core_ids=[0])
    got = tuple(r.results[0][f"out_{i}_dram"] for i in range(len(_OUTS)))
    return got[0]
```
